# Optimizing a Trainium2 kernel written in Bass

```python
import jax, jax.numpy as jnp
from jax import lax
import numpy as np
import math

D_MODEL = 1024
BATCH = 1
SEQ = 512
DEPTH = 1

POOL_WINDOWS = (2, 4, 8, 16)
POOL_GROUPS = len(POOL_WINDOWS)
POOL_GROUP_DIM = D_MODEL // 16
POOL_WIDTH = POOL_GROUPS * POOL_GROUP_DIM
ATTN_PATTERNS = ((128, 1), (512, 4), (2048, 16))
N_ATTN_GROUPS = len(ATTN_PATTERNS)
HEAD_DIM = 64
HEADS_PER_GROUP = 4
N_ATTN_HEADS = N_ATTN_GROUPS * HEADS_PER_GROUP
ATTN_WIDTH = N_ATTN_HEADS * HEAD_DIM
ATTN_OUT_WIDTH = HEADS_PER_GROUP * HEAD_DIM
ROPE_THETA = 10000.0
BLOCK = 128
N_BRANCHES = 2
IN_WIDTH = POOL_WIDTH + 3 * ATTN_WIDTH + N_BRANCHES * D_MODEL
D_FF = ((8 * D_MODEL // 3 + 255) // 256) * 256
N_MOD = 9
EPS = 1e-6


def rmsnorm(x, g):
    xf = x.astype(jnp.float32)
    y = xf * lax.rsqrt(jnp.mean(xf * xf, axis=-1, keepdims=True) + EPS)
    return (y * g.astype(jnp.float32)).astype(x.dtype)

def modulate(x, shift, scale):
    return x * (1 + scale) + shift

def swiglu(u, w_in, w_out):
    a, b = jnp.split(u @ w_in, 2, axis=-1)
    return (jax.nn.silu(a) * b) @ w_out

def rope_tables(positions, dtype):
    inv_freq = ROPE_THETA ** (-jnp.arange(0, HEAD_DIM, 2, dtype=jnp.float32) / HEAD_DIM)
    ang = positions.astype(jnp.float32)[..., None] * inv_freq
    return jnp.cos(ang)[:, :, None, :].astype(dtype), jnp.sin(ang)[:, :, None, :].astype(dtype)

def apply_rope(t, cos, sin):
    t1, t2 = jnp.split(t, 2, axis=-1)
    return jnp.concatenate([t1 * cos - t2 * sin, t2 * cos + t1 * sin], axis=-1)

def multiscale_pool(p, w_pool, pool_scale):
    B, S, _ = p.shape
    pf = p.astype(jnp.float32)
    cs = jnp.pad(jnp.cumsum(pf, axis=1), ((0, 0), (1, 0), (0, 0)))
    t = jnp.arange(S)
    outs = []
    for gi, w in enumerate(POOL_WINDOWS):
        sl = slice(gi * POOL_GROUP_DIM, (gi + 1) * POOL_GROUP_DIM)
        csg = cs[..., sl]
        lagged = jnp.pad(csg[:, :S + 1 - w], ((0, 0), (w - 1, 0), (0, 0)))
        count = jnp.minimum(t + 1, w).astype(jnp.float32)[None, :, None]
        outs.append((csg[:, 1:] - lagged) / count - pf[..., sl])
    d = jnp.stack(outs, axis=2).astype(p.dtype)
    y = jnp.einsum('bsgc,gcd->bsgd', d, w_pool)
    return y.reshape(B, S, POOL_WIDTH) * pool_scale

def dilated_window_attention(q, k, v, steps, dilation):
    B, S, H, Dh = q.shape
    L = S // dilation
    nb = -(-L // BLOCK)
    Lp = nb * BLOCK

    def to_strided(t):
        t = t.reshape(B, L, dilation, H, Dh).transpose(0, 3, 2, 1, 4)
        return jnp.pad(t, ((0, 0), (0, 0), (0, 0), (0, Lp - L), (0, 0)))

    qs, ks, vs = to_strided(q), to_strided(k), to_strided(v)
    qb = qs.reshape(B, H, dilation, nb, BLOCK, Dh)

    def band(t):
        tp = jnp.pad(t, ((0, 0), (0, 0), (0, 0), (BLOCK, 0), (0, 0)))
        prev = tp[..., :Lp, :].reshape(B, H, dilation, nb, BLOCK, Dh)
        cur = t.reshape(B, H, dilation, nb, BLOCK, Dh)
        return jnp.concatenate([prev, cur], axis=-2)

    kb, vb = band(ks), band(vs)
    a = jnp.arange(BLOCK)[:, None]
    cidx = jnp.arange(2 * BLOCK)[None, :]
    rel = a + BLOCK - cidx
    in_band = (rel >= 0) & (rel <= steps)
    key_pos = jnp.arange(nb)[:, None, None] * BLOCK - BLOCK + cidx[None]
    mask = in_band[None] & (key_pos >= 0)

    s = jnp.einsum('bhrnqd,bhrnkd->bhrnqk', qb, kb).astype(jnp.float32) * (HEAD_DIM ** -0.5)
    s = jnp.where(mask, s, -jnp.inf)
    lse = jax.nn.logsumexp(s, axis=-1)
    pr = jnp.exp(s - lse[..., None]).astype(v.dtype)
    o = jnp.einsum('bhrnqk,bhrnkd->bhrnqd', pr, vb)
    o = o.reshape(B, H, dilation, Lp, Dh)[:, :, :, :L]
    o = o.transpose(0, 3, 2, 1, 4).reshape(B, S, H, Dh)
    lse = lse.reshape(B, H, dilation, Lp)[:, :, :, :L].transpose(0, 3, 2, 1).reshape(B, S, H)
    return o, lse

def token_mixing(u, cos, sin, w_in, w_pool, pool_scale, w_pool_branch, w_attn_branch, w_out):
    B, S, _ = u.shape
    proj = u @ w_in
    cuts = [POOL_WIDTH, POOL_WIDTH + ATTN_WIDTH, POOL_WIDTH + 2 * ATTN_WIDTH,
            POOL_WIDTH + 3 * ATTN_WIDTH]
    p, q, k, v, gate_logits = jnp.split(proj, cuts, axis=-1)

    y_pool = multiscale_pool(p, w_pool, pool_scale)

    q = apply_rope(q.reshape(B, S, N_ATTN_HEADS, HEAD_DIM), cos, sin)
    k = apply_rope(k.reshape(B, S, N_ATTN_HEADS, HEAD_DIM), cos, sin)
    v = v.reshape(B, S, N_ATTN_HEADS, HEAD_DIM)
    outs, lses = [], []
    for gi, (window, dilation) in enumerate(ATTN_PATTERNS):
        hs = slice(gi * HEADS_PER_GROUP, (gi + 1) * HEADS_PER_GROUP)
        o, lse = dilated_window_attention(q[:, :, hs], k[:, :, hs], v[:, :, hs],
                                          window // dilation, dilation)
        outs.append(o)
        lses.append(lse)
    wts = jax.nn.softmax(jnp.stack(lses, axis=0), axis=0)
    y_attn = jnp.einsum('gbsh,gbshd->bshd', wts.astype(v.dtype), jnp.stack(outs, axis=0))
    y_attn = y_attn.reshape(B, S, ATTN_OUT_WIDTH)

    gates = jax.nn.sigmoid(gate_logits.astype(jnp.float32)).astype(u.dtype)
    g_pool, g_attn = jnp.split(gates, N_BRANCHES, axis=-1)
    merged = g_pool * (y_pool @ w_pool_branch) + g_attn * (y_attn @ w_attn_branch)
    return merged @ w_out

def first_inputs(seed: int = 0) -> dict:
    key = jax.random.key(seed)
    ks = jax.random.split(key, 20)
    f32 = jnp.float32

    def lin(k, shape, fan_in, scale=1.0):
        return jax.random.normal(k, shape, f32) * (scale * fan_in ** -0.5)

    def gain(k, shape):
        return 1.0 + 0.05 * jax.random.normal(k, shape, f32)

    x = jax.random.normal(ks[0], (BATCH, SEQ, D_MODEL), f32)
    c = jax.random.normal(ks[1], (BATCH, D_MODEL), f32)
    offset = jax.random.randint(ks[2], (BATCH, 1), 0, 1024, dtype=jnp.int32)
    positions = (jnp.arange(SEQ, dtype=jnp.int32)[None, :] + offset).astype(jnp.int32)
    return {
        "x": x,
        "c": c,
        "positions": positions,
        "w_ada": lin(ks[3], (DEPTH, D_MODEL, N_MOD * D_MODEL), D_MODEL, 0.5),
        "b_ada": 0.02 * jax.random.normal(ks[4], (DEPTH, N_MOD * D_MODEL), f32),
        "g_norm_ffn1": gain(ks[5], (DEPTH, D_MODEL)),
        "w_ffn1_in": lin(ks[6], (DEPTH, D_MODEL, 2 * D_FF), D_MODEL),
        "w_ffn1_out": lin(ks[7], (DEPTH, D_FF, D_MODEL), D_FF),
        "g_norm_mix": gain(ks[8], (DEPTH, D_MODEL)),
        "w_in": lin(ks[9], (DEPTH, D_MODEL, IN_WIDTH), D_MODEL),
        "w_pool": lin(ks[10], (DEPTH, POOL_GROUPS, POOL_GROUP_DIM, POOL_GROUP_DIM), POOL_GROUP_DIM),
        "pool_scale": 1.0 + 0.1 * jax.random.normal(ks[11], (DEPTH, POOL_WIDTH), f32),
        "w_pool_branch": lin(ks[12], (DEPTH, POOL_WIDTH, D_MODEL), POOL_WIDTH),
        "w_attn_branch": lin(ks[13], (DEPTH, ATTN_OUT_WIDTH, D_MODEL), ATTN_OUT_WIDTH),
        "w_out": lin(ks[14], (DEPTH, D_MODEL, D_MODEL), D_MODEL),
        "g_norm_ffn2": gain(ks[15], (DEPTH, D_MODEL)),
        "w_ffn2_in": lin(ks[16], (DEPTH, D_MODEL, 2 * D_FF), D_MODEL),
        "w_ffn2_out": lin(ks[17], (DEPTH, D_FF, D_MODEL), D_FF),
        "g_final": gain(ks[18], (D_MODEL,)),
    }

def first_block(x, c, positions, w_ada, b_ada, g_norm_ffn1, w_ffn1_in, w_ffn1_out,
              g_norm_mix, w_in, w_pool, pool_scale, w_pool_branch, w_attn_branch, w_out,
              g_norm_ffn2, w_ffn2_in, w_ffn2_out, g_final):
    cos, sin = rope_tables(positions, x.dtype)
    cond = jax.nn.silu(c)
    h = x
    for l in range(DEPTH):
        mod = cond @ w_ada[l] + b_ada[l]
        sh1, sc1, gt1, sh2, sc2, gt2, sh3, sc3, gt3 = [
            m[:, None, :] for m in jnp.split(mod, N_MOD, axis=-1)]
        u = modulate(rmsnorm(h, g_norm_ffn1[l]), sh1, sc1)
        h = h + 0.5 * gt1 * swiglu(u, w_ffn1_in[l], w_ffn1_out[l])
        u = modulate(rmsnorm(h, g_norm_mix[l]), sh2, sc2)
        h = h + gt2 * token_mixing(u, cos, sin, w_in[l], w_pool[l], pool_scale[l],
                                   w_pool_branch[l], w_attn_branch[l], w_out[l])
        u = modulate(rmsnorm(h, g_norm_ffn2[l]), sh3, sc3)
        h = h + 0.5 * gt3 * swiglu(u, w_ffn2_in[l], w_ffn2_out[l])
    return rmsnorm(h, g_final)


DEPTH_2 = 2

N_MIXERS = 2
N_CONV_LAYERS = (DEPTH_2 + N_MIXERS - 1) // N_MIXERS
N_ATTN_LAYERS = DEPTH_2 // N_MIXERS
CONV_WIDTH = 3
N_HEADS = 16
KV_LATENT = 128
N_IDX_HEADS = 8
IDX_DIM = 64
TOPK_MAX = 256
Q_BLOCK = 128
ATTN_IN_WIDTH = N_HEADS * KV_LATENT + KV_LATENT + N_IDX_HEADS * IDX_DIM + IDX_DIM + N_IDX_HEADS
N_BUCKETS = 32
MAX_DISTANCE = 128
N_GROUPS = 8
EXPERTS_PER_GROUP = 8
N_EXPERTS = N_GROUPS * EXPERTS_PER_GROUP
TOPK_IN_GROUP = 2
D_EXPERT = 256
MOE_BLOCK = 128
LN_EPS = 1e-5
RMS_EPS = 1e-6
DEEPNORM_ALPHA = (2.0 * DEPTH_2) ** 0.25
DEEPNORM_BETA = (8.0 * DEPTH_2) ** -0.25


def layer_norm(x, g, b):
    xf = x.astype(jnp.float32)
    mu = jnp.mean(xf, axis=-1, keepdims=True)
    var = jnp.mean(jnp.square(xf - mu), axis=-1, keepdims=True)
    y = (xf - mu) * lax.rsqrt(var + LN_EPS) * g.astype(jnp.float32) + b.astype(jnp.float32)
    return y.astype(x.dtype)

def rms_norm(x, g):
    xf = x.astype(jnp.float32)
    y = xf * lax.rsqrt(jnp.mean(jnp.square(xf), axis=-1, keepdims=True) + RMS_EPS) * g.astype(jnp.float32)
    return y.astype(x.dtype)

def t5_bucket(dist):
    max_exact = N_BUCKETS // 2
    d_f = jnp.maximum(dist, 1).astype(jnp.float32)
    large = max_exact + (jnp.log(d_f / max_exact) / math.log(MAX_DISTANCE / max_exact)
                         * (N_BUCKETS - max_exact)).astype(jnp.int32)
    large = jnp.minimum(large, N_BUCKETS - 1)
    return jnp.where(dist < max_exact, dist, large)

def short_conv_mixer(x, w_in, conv_k, w_out):
    S = x.shape[1]
    b_gate, c_gate, h = jnp.split(x @ w_in, 3, axis=-1)
    u = c_gate * h
    up = jnp.pad(u, ((0, 0), (CONV_WIDTH - 1, 0), (0, 0)))
    conv = up[:, 0:S] * conv_k[0]
    for j in range(1, CONV_WIDTH):
        conv = conv + up[:, j:j + S] * conv_k[j]
    return (b_gate * conv) @ w_out

def dsa_mixer(x, w_in, kv_norm_g, kidx_ln_g, kidx_ln_b, w_out, rel_bias):
    Bsz, S, _ = x.shape
    topk = min(TOPK_MAX, S // 4)
    hq = N_HEADS * KV_LATENT
    cuts = [hq, hq + KV_LATENT, hq + KV_LATENT + N_IDX_HEADS * IDX_DIM,
            hq + KV_LATENT + N_IDX_HEADS * IDX_DIM + IDX_DIM]
    q, c_kv, q_idx, k_idx, w_idx = jnp.split(x @ w_in, cuts, axis=-1)
    q = q.reshape(Bsz, S, N_HEADS, KV_LATENT)
    c_kv = rms_norm(c_kv, kv_norm_g)
    q_idx = q_idx.reshape(Bsz, S, N_IDX_HEADS, IDX_DIM)
    k_idx = layer_norm(k_idx, kidx_ln_g, kidx_ln_b)
    w_idx = w_idx * (N_IDX_HEADS ** -0.5)
    nb = S // Q_BLOCK
    key_pos = jnp.arange(S)

    def to_blocks(a):
        return jnp.moveaxis(a.reshape(Bsz, nb, Q_BLOCK, *a.shape[2:]), 1, 0)

    def block_fn(args):
        qb, qib, wb, blk = args
        t = blk * Q_BLOCK + jnp.arange(Q_BLOCK)
        s_idx = jnp.einsum('bthd,bsd->bths', qib, k_idx,
                           preferred_element_type=jnp.float32) * (IDX_DIM ** -0.5)
        score = jnp.einsum('bths,bth->bts', jax.nn.relu(s_idx), wb.astype(jnp.float32))
        causal = key_pos[None, :] <= t[:, None]
        score = jnp.where(causal[None], score, -jnp.inf)
        _, sel = lax.top_k(score, topk)
        valid = sel <= t[None, :, None]
        kv_sel = jax.vmap(lambda c, i: c[i])(c_kv, sel)
        logits = jnp.einsum('bthc,btjc->bthj', qb, kv_sel,
                            preferred_element_type=jnp.float32) * (KV_LATENT ** -0.5)
        bucket = t5_bucket(jnp.maximum(t[None, :, None] - sel, 0))
        bias = jnp.moveaxis(rel_bias[bucket], -1, 2)
        logits = logits + bias.astype(jnp.float32)
        logits = jnp.where(valid[:, :, None, :], logits, -jnp.inf)
        p = jax.nn.softmax(logits, axis=-1).astype(x.dtype)
        o = jnp.einsum('bthj,btjc->bthc', p, kv_sel)
        return o.reshape(Bsz, Q_BLOCK, hq)

    o = lax.map(block_fn, (to_blocks(q), to_blocks(q_idx), to_blocks(w_idx), jnp.arange(nb)))
    o = jnp.moveaxis(o, 0, 1).reshape(Bsz, S, hq)
    return o @ w_out

def hier_moe(x, wg, bg, we, be, w1, w3, w2):
    Bsz, S, D = x.shape
    xt = x.reshape(-1, D)
    T = xt.shape[0]
    g_logits = (xt @ wg + bg).astype(jnp.float32)
    g_prob = jax.nn.softmax(g_logits, axis=-1)
    g_top = jnp.argmax(g_logits, axis=-1)
    g_gate = jnp.take_along_axis(g_prob, g_top[:, None], axis=-1)
    e_logits = (xt @ we + be).astype(jnp.float32).reshape(T, N_GROUPS, EXPERTS_PER_GROUP)
    e_logits = jnp.take_along_axis(e_logits, g_top[:, None, None], axis=1)[:, 0]
    e_val, e_loc = lax.top_k(e_logits, TOPK_IN_GROUP)
    gate = jax.nn.softmax(e_val, axis=-1) * g_gate
    e_id = g_top[:, None] * EXPERTS_PER_GROUP + e_loc
    N = T * TOPK_IN_GROUP
    flat_e = e_id.reshape(-1).astype(jnp.int32)
    flat_tok = jnp.repeat(jnp.arange(T, dtype=jnp.int32), TOPK_IN_GROUP)
    flat_w = gate.reshape(-1)
    order = jnp.argsort(flat_e)
    e_s, tok_s, w_s = flat_e[order], flat_tok[order], flat_w[order]
    counts = jax.ops.segment_sum(jnp.ones_like(flat_e), flat_e, num_segments=N_EXPERTS)
    padded = (counts + MOE_BLOCK - 1) // MOE_BLOCK * MOE_BLOCK
    start = jnp.cumsum(counts) - counts
    pend = jnp.cumsum(padded)
    pstart = pend - padded
    dest = pstart[e_s] + jnp.arange(N, dtype=jnp.int32) - start[e_s]
    R = (-(-N // MOE_BLOCK) + N_EXPERTS) * MOE_BLOCK
    row_tok = jnp.zeros((R,), jnp.int32).at[dest].set(tok_s)
    row_w = jnp.zeros((R,), jnp.float32).at[dest].set(w_s)
    nblk = R // MOE_BLOCK
    blk_e = jnp.minimum(jnp.searchsorted(pend, jnp.arange(nblk, dtype=jnp.int32) * MOE_BLOCK,
                                         side='right'), N_EXPERTS - 1)
    xs = xt[row_tok].reshape(nblk, MOE_BLOCK, D)

    def expert_block(args):
        xb, e = args
        h = jax.nn.silu(xb @ w1[e]) * (xb @ w3[e])
        return h @ w2[e]

    ys = lax.map(expert_block, (xs, blk_e)).reshape(R, D)
    out = jnp.zeros_like(xt).at[row_tok].add(ys * row_w[:, None].astype(ys.dtype))
    return out.reshape(Bsz, S, D)

def second_inputs(seed: int = 0) -> dict:
    key = jax.random.key(seed)
    ks = jax.random.split(key, 24)
    D = D_MODEL
    f32 = jnp.float32

    def nrm(k, shape, scale):
        return jax.random.normal(k, shape, f32) * scale

    return {
        "x": nrm(ks[0], (BATCH, SEQ, D), 1.0),
        "conv_w_in": nrm(ks[1], (N_CONV_LAYERS, D, 3 * D), D ** -0.5),
        "conv_k": nrm(ks[2], (N_CONV_LAYERS, CONV_WIDTH, D), CONV_WIDTH ** -0.5),
        "conv_w_out": nrm(ks[3], (N_CONV_LAYERS, D, D), DEEPNORM_BETA * D ** -0.5),
        "attn_w_in": nrm(ks[4], (N_ATTN_LAYERS, D, ATTN_IN_WIDTH), D ** -0.5),
        "kv_norm_g": 1.0 + nrm(ks[5], (N_ATTN_LAYERS, KV_LATENT), 0.02),
        "kidx_ln_g": 1.0 + nrm(ks[6], (N_ATTN_LAYERS, IDX_DIM), 0.02),
        "kidx_ln_b": nrm(ks[7], (N_ATTN_LAYERS, IDX_DIM), 0.02),
        "attn_w_out": nrm(ks[8], (N_ATTN_LAYERS, N_HEADS * KV_LATENT, D),
                          DEEPNORM_BETA * (N_HEADS * KV_LATENT) ** -0.5),
        "rel_bias": nrm(ks[9], (N_BUCKETS, N_HEADS), 0.5),
        "router_wg": nrm(ks[10], (DEPTH_2, D, N_GROUPS), D ** -0.5),
        "router_bg": nrm(ks[11], (DEPTH_2, N_GROUPS), 0.01),
        "router_we": nrm(ks[12], (DEPTH_2, D, N_EXPERTS), D ** -0.5),
        "router_be": nrm(ks[13], (DEPTH_2, N_EXPERTS), 0.01),
        "exp_w1": nrm(ks[14], (DEPTH_2, N_EXPERTS, D, D_EXPERT), D ** -0.5),
        "exp_w3": nrm(ks[15], (DEPTH_2, N_EXPERTS, D, D_EXPERT), D ** -0.5),
        "exp_w2": nrm(ks[16], (DEPTH_2, N_EXPERTS, D_EXPERT, D), DEEPNORM_BETA * D_EXPERT ** -0.5),
        "ln1_g": 1.0 + nrm(ks[17], (DEPTH_2, D), 0.02),
        "ln1_b": nrm(ks[18], (DEPTH_2, D), 0.02),
        "ln2_g": 1.0 + nrm(ks[19], (DEPTH_2, D), 0.02),
        "ln2_b": nrm(ks[20], (DEPTH_2, D), 0.02),
    }

def second_block(x, conv_w_in, conv_k, conv_w_out, attn_w_in, kv_norm_g, kidx_ln_g, kidx_ln_b,
              attn_w_out, rel_bias, router_wg, router_bg, router_we, router_be,
              exp_w1, exp_w3, exp_w2, ln1_g, ln1_b, ln2_g, ln2_b):
    for i in range(DEPTH_2):
        j = i // N_MIXERS
        if i % N_MIXERS == 0:
            m = short_conv_mixer(x, conv_w_in[j], conv_k[j], conv_w_out[j])
        else:
            m = dsa_mixer(x, attn_w_in[j], kv_norm_g[j], kidx_ln_g[j], kidx_ln_b[j],
                          attn_w_out[j], rel_bias)
        x = layer_norm(DEEPNORM_ALPHA * x + m, ln1_g[i], ln1_b[i])
        f = hier_moe(x, router_wg[i], router_bg[i], router_we[i], router_be[i],
                     exp_w1[i], exp_w3[i], exp_w2[i])
        x = layer_norm(DEEPNORM_ALPHA * x + f, ln2_g[i], ln2_b[i])
    return x


def setup_inputs(seed=0):
    out = dict(first_inputs(seed))
    for name, value in second_inputs(seed + 1).items():
        if name != "x":
            out[name + "_2"] = value
    return out


def reference(
    x, c, positions, w_ada, b_ada, g_norm_ffn1, w_ffn1_in, w_ffn1_out, g_norm_mix, w_in, w_pool,
    pool_scale, w_pool_branch, w_attn_branch, w_out, g_norm_ffn2, w_ffn2_in, w_ffn2_out,
    g_final, conv_w_in_2, conv_k_2, conv_w_out_2, attn_w_in_2, kv_norm_g_2, kidx_ln_g_2,
    kidx_ln_b_2, attn_w_out_2, rel_bias_2, router_wg_2, router_bg_2, router_we_2, router_be_2,
    exp_w1_2, exp_w3_2, exp_w2_2, ln1_g_2, ln1_b_2, ln2_g_2, ln2_b_2,
):
    x = first_block(
        x, c, positions, w_ada, b_ada, g_norm_ffn1, w_ffn1_in, w_ffn1_out, g_norm_mix, w_in,
        w_pool, pool_scale, w_pool_branch, w_attn_branch, w_out, g_norm_ffn2, w_ffn2_in,
        w_ffn2_out, g_final,
    )
    return second_block(
        x, conv_w_in_2, conv_k_2, conv_w_out_2, attn_w_in_2, kv_norm_g_2, kidx_ln_g_2,
        kidx_ln_b_2, attn_w_out_2, rel_bias_2, router_wg_2, router_bg_2, router_we_2,
        router_be_2, exp_w1_2, exp_w3_2, exp_w2_2, ln1_g_2, ln1_b_2, ln2_g_2, ln2_b_2,
    )


_drawn_inputs = setup_inputs


def setup_inputs(seed=0):
    import zlib

    import numpy as np

    out = dict(_drawn_inputs(seed))
    spreads = {}
    factors = {'g_norm_ffn1': 4.297,
     'g_norm_mix': 4.205,
     'pool_scale': 2.729,
     'g_norm_ffn2': 4.483,
     'kv_norm_g_2': 8.0,
     'kidx_ln_g_2': 8.0,
     'kidx_ln_b_2': 8.0,
     'router_bg_2': 6.78,
     'router_be_2': 8.0}
    for name, (base, spread) in spreads.items():
        noise = np.random.default_rng([zlib.crc32(name.encode()), seed]).standard_normal(out[name].shape)
        drawn = base * np.exp(spread * noise) if base else spread * noise
        out[name] = __import__('jax').numpy.asarray(drawn.astype(out[name].dtype))
    for name, factor in factors.items():
        out[name] = (out[name] * factor).astype(out[name].dtype)
    return out
```

```python
from contextlib import ExitStack

import numpy as np

import concourse.bass as bass
from concourse import mybir

F32 = mybir.dt.float32
I32 = mybir.dt.int32
U32 = mybir.dt.uint32
ALU = mybir.AluOpType
ACT = mybir.ActivationFunctionType
AXX = mybir.AxisListType.X

P = 128
SEQ = 512
D = 1024
KT = D // P
TT = SEQ // P
FF = 2816
FT = FF // P
HEAD = 64
POOL_W = 256
ATT_W = 768
N_MOD = 9
CLASSES = 4
RMS_EPS = 1e-6
LN_EPS = 1e-5
ALPHA = (2.0 * 2) ** 0.25
NEG = -1e30
TAKEN = -3e38
IDX_HEADS = 8
IDX_DIM = 64
LATENT = 128
HEADS2 = 16
TOPK = SEQ // 4
BUCKETS = 32
EXPERTS = 64
GROUPS = 8
PER_GROUP = 8
D_EXP = 256
PAIRS = 2 * SEQ
WIN = 64
SLOTS = PAIRS + WIN
MAX_ROUNDS = SEQ // WIN
RING = 6
CHUNK = 2048

PC = {}
_at = 0
for _name, _n in (("b_ada", 72), ("g_ffn1", 8), ("g_mix", 8), ("g_ffn2", 8), ("g_final", 8), ("c", 8),
                  ("pool_scale", 2), ("conv_k", 24), ("ln1_g", 16), ("ln1_b", 16), ("ln2_g", 16), ("ln2_b", 16)):
    PC[_name] = _at
    _at += _n
N_PARAM = _at

CC = {}
_at = 0
for _name, _n in (("ident", P), ("causal", P), ("before", P), ("slot", PAIRS), ("lane", 2 * WIN), ("invf", 1),
                  ("rot", P), ("mod4", P), ("band", CLASSES * SEQ), ("recip", 2 * SEQ), ("bucket", 640)):
    CC[_name] = _at
    _at += _n
N_CONST = _at
N_KEEP = CC["rot"]


def constants():
    c = np.zeros((P, N_CONST), np.float32)
    p = np.arange(P)[:, None]
    q = np.arange(P)[None, :]

    def put(name, a):
        c[:a.shape[0], CC[name]:CC[name] + a.shape[1]] = a

    put("ident", (p == q).astype(np.float32))
    put("causal", np.where(q <= p, 0.0, NEG))
    put("before", (p < q).astype(np.float32))
    put("slot", np.broadcast_to(np.arange(PAIRS), (P, PAIRS)))
    put("lane", np.broadcast_to(np.arange(2 * WIN) % WIN, (P, 2 * WIN)))
    rot = np.zeros((P, P))
    for m in range(P):
        if m % HEAD < HEAD // 2:
            rot[m + HEAD // 2, m] = -1.0
        else:
            rot[m - HEAD // 2, m] = 1.0
    put("rot", rot)
    put("mod4", np.where((q <= p) & ((p - q) % 4 == 0), 0.0, NEG))
    s = np.arange(SEQ)[None, :]
    for k in range(CLASSES):
        d = k + CLASSES * p - s
        c[:, CC["band"] + k * SEQ:CC["band"] + (k + 1) * SEQ] = np.where((d >= 0) & (d <= 128), 0.0, NEG)
    t = np.arange(SEQ)
    for tile in range(2):
        for half in range(2):
            w = 2 ** (1 + 2 * tile + half)
            at = CC["recip"] + tile * SEQ
            c[64 * half:64 * half + 64, at:at + SEQ] = (np.float32(1) / np.minimum(t + 1, w).astype(np.float32))[None]
    inv = np.float32(10000.0) ** (-np.arange(0, HEAD, 2, dtype=np.float32) / np.float32(HEAD))
    c[:, CC["invf"]] = np.tile(inv, P // 32)
    dist = np.maximum(SEQ - 1 - np.arange(640), 0)
    large = 16 + (np.log(np.maximum(dist, 1).astype(np.float32) / np.float32(16)) / np.float32(np.log(8.0))
                  * np.float32(16)).astype(np.int32)
    bucket = np.where(dist < 16, dist, np.minimum(large, BUCKETS - 1))
    put("bucket", (np.arange(BUCKETS)[:, None] == bucket[None, :]).astype(np.float32))
    return c


class Steps:

    def __init__(self, eng, sem):
        self.eng, self.sem, self.n = eng, sem, 0

    def did(self, ins):
        self.n += 1
        ins.then_inc(self.sem, 1)

    def wait(self):
        self.eng.wait_ge(self.sem, self.n)


def build(nc, A, out):
    with ExitStack() as ctx:
        def sb(name, shape, dt=F32):
            return ctx.enter_context(nc.sbuf_tensor(name, shape, dt))

        _sems = {}

        def sem(name):
            if name not in _sems:
                _sems[name] = ctx.enter_context(nc.semaphore(name))
            return _sems[name]

        H = sb("H", [P, KT, SEQ])
        U = sb("U", [P, KT, SEQ])
        ring = sb("ring", [P, RING, CHUNK])
        keep = sb("keep", [P, N_KEEP])
        par = sb("par", [P, N_PARAM])
        mod = sb("mod", [P, 72])
        gains = sb("gains", [P, 24])
        gates = sb("gates", [P, 24])
        csil = sb("csil", [P, KT])
        kvg = sb("kvg", [P, LATENT])
        lng = sb("lng", [P, IDX_DIM])
        lnb = sb("lnb", [P, IDX_DIM])
        rbias = sb("rbias", [P, 2, 72])
        rw = sb("rw", [P, 2, KT, 72])
        ones = sb("ones", [P, P])
        epsc = sb("epsc", [P, 3])
        rstd = sb("rstd", [P, SEQ])
        small = sb("small", [P, 64])
        arena = sb("arena", [P, 28544])
        bank = [ctx.enter_context(nc.psum_tensor(f"bank{i}", [P, 512], F32)) for i in range(8)]

        ident = keep[:, CC["ident"]:CC["ident"] + P]
        causal = keep[:, CC["causal"]:CC["causal"] + P]
        before = keep[:, CC["before"]:CC["before"] + P]
        slotrow = keep[:, CC["slot"]:CC["slot"] + PAIRS]
        invf = keep[:, CC["invf"]:CC["invf"] + 1]
        lane = keep[:, CC["lane"]:CC["lane"] + 2 * WIN]

        def area(at, *shape):
            n = int(np.prod(shape))
            assert at + n <= 28544, (at, shape)
            v = arena[:, at:at + n]
            if len(shape) == 2:
                v = v.rearrange("p (a b) -> p a b", a=shape[0])
            if len(shape) == 3:
                v = v.rearrange("p (a b c) -> p a b c", a=shape[0], b=shape[1])
            return v

        def col(name, i=0):
            return par[:, PC[name] + i:PC[name] + i + 1]

        spread = nc.dram_tensor("bias_spread", [P, HEADS2, 640], F32, kind="Internal").ap()
        scratch = nc.dram_tensor("bias_rows", [HEADS2, 640], F32, kind="Internal").ap()

        xtok = area(0, TT, D)
        G = area(0, FT, SEQ)
        Q = area(0, 6, SEQ)
        K = area(3072, 6, SEQ)
        MG = area(0, KT, SEQ)
        V = area(6144, 3, TT, 256)
        S1 = area(9216, 2, 768)
        PT1 = area(10752, 6, P)
        PB = area(9216, 2, 528)
        PS2 = area(10272, 2, 528)
        PS4 = area(11328, 2, 528)
        PRC = area(12384, 2, SEQ)
        PD = area(13408, 2, SEQ)
        GT = area(14432, 16, SEQ)
        cosT = area(22624, SEQ)
        sinT = area(23136, SEQ)
        band = area(23648, CLASSES, SEQ)
        mod4 = area(25696, P)
        rotm = area(25824, P)
        wpool = area(25952, 2, P)
        YA = area(26208, 2, SEQ)
        YP = area(27232, 2, SEQ)
        RT = area(26208, 2, SEQ)
        RT2 = area(9216, SEQ)
        posi = arena[:, 0:SEQ].bitcast(I32)
        TB = area(512, 6, SEQ)
        CG = area(0, 2, SEQ)
        CU = area(1024, 2, SEQ + 2)
        CV = area(2056, 2, SEQ)
        BC = area(3080, KT, SEQ)
        XT = area(0, TT, D)
        SEL = area(4096, TT, PAIRS)
        YST = area(0, KT, SLOTS)
        XST = area(8704, KT, SLOTS)
        SELW = area(17408, TT, PAIRS)
        XW = area(21504, 2, KT, WIN)
        SA = area(22528, 2, 2 * WIN)
        HB = area(22784, 2, 2 * WIN)
        HM = area(23040, 2, 2 * WIN)
        YS = area(8704, 8, D)
        SWT = area(23296, 8, SEQ)
        LG = area(23296, TT, 72)
        RK = area(23600, 2048)
        SELT = area(25648, PAIRS)
        REM = area(27392, MAX_ROUNDS * EXPERTS)
        startf = area(27904, EXPERTS)
        STI = arena[:, 27968:27968 + MAX_ROUNDS * EXPERTS].bitcast(I32)
        plan = arena[:, 28480:28484].bitcast(I32)
        Q2 = area(0, HEADS2, SEQ)
        TOE = area(8192, HEADS2, SEQ)
        CKV = area(16384, TT, LATENT)
        CKVT = area(16896, SEQ)
        SM = area(17408, 3, SEQ)
        QI = area(18944, 4, SEQ)
        KI = area(20992, TT, P)
        KIT = area(21504, SEQ)
        IR = area(22016, 2, SEQ)
        S2 = area(23040, 2, SEQ)
        PT2 = area(24064, 2, SEQ)
        VB = area(25088, 640)
        BKT = area(25728, 640)
        RB = area(26368, 16)
        W8 = area(26384, TT, 8)
        DS = area(26416, 512)

        def tall(w, c0, n):
            return w[:, c0:c0 + n].rearrange("(k p) n -> p k n", p=P)

        def flat(w, k0, nk, c0, n):
            return w[k0 * P:(k0 + nk) * P, c0:c0 + n].rearrange("(k p) n -> p k n", p=P)

        stream_a, stream_b = [], []
        first = {}

        def outs(stream, name, w, kts):
            first[name] = len(stream)
            n = 0
            for half in range(2):
                for k0 in range(0, kts, 4):
                    n += 1
                    nk = min(4, kts - k0)
                    stream.append((flat(w, k0, nk, 512 * half, 512), nk, 512, name + "_used", n))

        first["ada"] = 0
        for c in range(36):
            stream_a.append((tall(A["w_ada"], 256 * c, 256), KT, 256, "ada_used", c + 1))

        def ffn_stream(i):
            first[f"ffn{i}"] = len(stream_a)
            w = A[f"w_ffn{i + 1}_in"]
            for c in range(FT // 2):
                stream_a.append((tall(w, 256 * c, 256), KT, 256, "ffn_a", FT * i + 2 * c + 2))
                stream_a.append((tall(w, FF + 256 * c, 256), KT, 256, "ffn_b", FT * i + 2 * c + 2))
            outs(stream_a, f"ffn{i}_out", A[f"w_ffn{i + 1}_out"], FT)

        ffn_stream(0)
        first["mix"] = len(stream_a)
        mix_tiles = [2, 4, 6, 8, 10, 12, 14, 18, 22, 26] + [28 + 2 * i for i in range(8)]
        for c, n in enumerate(mix_tiles):
            stream_a.append((tall(A["w_in"], 256 * c, 256), KT, 256, "mix_tile", n))
        first["branch"] = len(stream_a)
        stream_a.append((flat(A["w_pool_branch"], 0, 2, 0, 1024), 2, 1024, "merge_ab", 8))
        stream_a.append((flat(A["w_attn_branch"], 0, 2, 0, 1024), 2, 1024, "merge_ab", 8))
        outs(stream_a, "mix_out", A["w_out"], KT)
        ffn_stream(1)
        first["conv"] = len(stream_a)
        for j in range(4):
            for which, at in enumerate((1024, 2048, 0)):
                stream_a.append((tall(A["conv_w_in"], at + 256 * j, 256), KT, 256,
                                 ("conv_c", "conv_h", "conv_b")[which], 2 * j + 2))
        outs(stream_a, "conv_out", A["conv_w_out"], KT)
        first["dsa"] = 0
        for n, c in enumerate((8, 9, 10)):
            stream_b.append((tall(A["attn_w_in"], 256 * c, 256 if c < 10 else 200), KT, 256 if c < 10 else 200,
                             ("qi_mm", "qi_mm", "ki_mm")[n], (1, 3, 1)[n]))
        for c in range(8):
            stream_b.append((tall(A["attn_w_in"], 256 * c, 256), KT, 256, "dsa_q", 2 * c + 2))
        outs(stream_b, "dsa_out", A["attn_w_out"], HEADS2)
        streams = {"a": stream_a, "b": stream_b}
        assert len(stream_a) % RING == 0

        def wview(slot, nk, n):
            return ring[:, slot, 0:nk * n].rearrange("p (k n) -> p k n", k=nk)

        def chunk(which, n):
            _, nk, cols, _, _ = streams[which][n]
            return wview(n % RING, nk, cols)

        def landed(eng, which, n, more=0):
            n += len(stream_a) if which == "b" else 0
            eng.wait_ge(sem(f"w_{n % RING}"), 16 * (n // RING + 1) + more)

        block = ctx.enter_context(nc.Block())

        @block.sync
        def _(sp):
            def load(which, n):
                src, nk, cols, _, _ = streams[which][n]
                sp.dma_start(wview(n % RING, nk, cols), src).then_inc(sem(f"w_{n % RING}"), 16)

            def experts(layer, i, pair0):
                for s in range(2):
                    e = pair0 * 2 + s
                    for j, w in enumerate(("exp_w1", "exp_w3", "exp_w2")):
                        one = A[w][layer, bass.ds(e, 1)] if not isinstance(e, int) else A[w][layer, e:e + 1]
                        src = one.rearrange("a (k p) n -> p (a k) n", p=P)
                        slot = 3 * s + j
                        nk, cols = (KT, D_EXP) if j < 2 else (2, D)
                        if i is not None:
                            sp.wait_ge(sem(f"moe{layer}_{'aby'[j]}"), i * 2 + (s - 1))
                        sp.dma_start(wview(slot, nk, cols), src).then_inc(sem(f"w_m{layer}{slot}"), 16)

            for n in range(len(stream_a)):
                if n >= RING:
                    _, _, _, s, v = stream_a[n - RING]
                    sp.wait_ge(sem(s), v)
                load("a", n)

            rounds = None
            for layer in range(2):
                prev = streams["ab"[layer]]
                used = {}
                for n in range(len(prev)):
                    used[n % RING] = prev[n][3:]
                for slot in range(RING):
                    s, v = used[slot]
                    sp.wait_ge(sem(s), v)
                    j = slot % 3
                    w = ("exp_w1", "exp_w3", "exp_w2")[j]
                    nk, cols = (KT, D_EXP) if j < 2 else (2, D)
                    sp.dma_start(wview(slot, nk, cols), A[w][layer, slot // 3].rearrange("(k p) n -> p k n", p=P))\
                      .then_inc(sem(f"w_m{layer}{slot}"), 16)
                sp.wait_ge(sem("moe_plan"), layer + 1)
                rounds = sp.value_load(plan[0:1, 0:1], min_val=1, max_val=MAX_ROUNDS)
                with sp.Fori(0, rounds) as j:
                    with sp.Fori(1, EXPERTS // 2) as i:
                        experts(layer, j * (EXPERTS // 2) + i, i)
                    with sp.If(j + 1 < rounds):
                        experts(layer, (j + 1) * (EXPERTS // 2), 0)
                if layer == 0:
                    last = sp.value_load(plan[0:1, 2:3], min_val=EXPERTS - 1, max_val=MAX_ROUNDS * EXPERTS - 1)
                    every = sp.value_load(plan[0:1, 3:4], min_val=EXPERTS, max_val=MAX_ROUNDS * EXPERTS)
                    for n in range(len(stream_b)):
                        if n < RING:
                            sp.wait_ge(sem(f"moe0_{'aby'[n % 3]}"), last if n < 3 else every)
                        else:
                            _, _, _, s, v = stream_b[n - RING]
                            sp.wait_ge(sem(s), v)
                        load("b", n)
            sp.wait_ge(sem("xt"), 24)
            sp.dma_start(out.rearrange("a (t p) d -> p (a t) d", p=P), XT).then_inc(sem("stored"), 16)
            sp.wait_ge(sem("stored"), 16)

        @block.gpsimd
        def _(pool):
            st = Steps(pool, sem("pool_step"))
            st.did(pool.memset(ones[:], 1.0))
            pool.memset(epsc[:, 0:1], RMS_EPS).then_inc(sem("eps"), 1)
            pool.memset(epsc[:, 1:2], LN_EPS).then_inc(sem("eps"), 1)
            pool.memset(epsc[:, 2:3], 0.0).then_inc(sem("eps"), 1)
            for l in range(2):
                pool.dma_start(rw[:, l, :, 0:GROUPS], A["router_wg"][l].rearrange("(k p) n -> p k n", p=P))\
                    .then_inc(sem("rows"), 16)
                pool.dma_start(rw[:, l, :, GROUPS:72], A["router_we"][l].rearrange("(k p) n -> p k n", p=P))\
                    .then_inc(sem("rows"), 16)
                pool.dma_start(rbias[:, l, 0:GROUPS], A["router_bg"][l].partition_broadcast(P)).then_inc(sem("rows"), 16)
                pool.dma_start(rbias[:, l, GROUPS:72], A["router_be"][l].partition_broadcast(P)).then_inc(sem("rows"), 16)
            pool.dma_start(kvg[:], A["kv_norm_g"][0].partition_broadcast(P)).then_inc(sem("rows"), 16)
            pool.dma_start(lng[:], A["kidx_ln_g"][0].partition_broadcast(P)).then_inc(sem("rows"), 16)
            pool.dma_start(lnb[:], A["kidx_ln_b"][0].partition_broadcast(P)).then_inc(sem("rows"), 16)

            pool.wait_ge(sem("h"), 8)
            mixc = sem("mix_const")
            for name, dst in (("rot", rotm), ("mod4", mod4)):
                pool.dma_start(dst, A["consts"][:, CC[name]:CC[name] + P]).then_inc(mixc, 16)
            pool.dma_start(band, A["consts"][:, CC["band"]:CC["band"] + CLASSES * SEQ]
                           .rearrange("p (a b) -> p a b", a=CLASSES)).then_inc(mixc, 16)
            pool.dma_start(PRC, A["consts"][:, CC["recip"]:CC["recip"] + 2 * SEQ]
                           .rearrange("p (a b) -> p a b", a=2)).then_inc(mixc, 16)
            pool.dma_start(posi, A["positions"][0].partition_broadcast(P)).then_inc(mixc, 16)
            st.did(pool.memset(wpool, 0.0))
            st.wait()
            for g in range(4):
                r = 64 * (g % 2)
                pool.dma_start(wpool[r:r + 64, g // 2, r:r + 64], A["w_pool"][g]).then_inc(sem("wpool"), 16)
            st.did(pool.memset(PB[:, :, 0:16], 0.0))
            st.did(pool.memset(PS2[:, :, 0:16], 0.0))
            st.did(pool.memset(PS4[:, :, 0:16], 0.0))
            pool.wait_ge(sem("mix_evac"), 2)
            pool.wait_ge(mixc, 80)
            st.wait()
            N = slice(16, 528)
            st.did(pool.tensor_tensor(PS2[:, :, N], PB[:, :, N], PB[:, :, 15:527], ALU.add))
            st.wait()
            st.did(pool.tensor_tensor(PS4[:, :, N], PS2[:, :, N], PS2[:, :, 14:526], ALU.add))
            st.wait()
            st.did(pool.tensor_tensor(PD[0:64, 0], PS2[0:64, 0, N], PRC[0:64, 0], ALU.mult))
            st.wait()
            st.did(pool.tensor_tensor(PD[64:P, 0], PS4[64:P, 0, N], PRC[64:P, 0], ALU.mult))
            st.wait()
            st.did(pool.tensor_tensor(PS2[:, 1, N], PS4[:, 1, N], PS4[:, 1, 12:524], ALU.add))
            st.wait()
            st.did(pool.tensor_tensor(PD[0:64, 1], PS2[0:64, 1, N], PRC[0:64, 1], ALU.mult))
            st.wait()
            st.did(pool.tensor_tensor(PS4[64:P, 1, N], PS2[64:P, 1, N], PS2[64:P, 1, 8:520], ALU.add))
            st.wait()
            st.did(pool.tensor_tensor(PD[64:P, 1], PS4[64:P, 1, N], PRC[64:P, 1], ALU.mult))
            st.wait()
            pool.tensor_tensor(PD, PD, PB[:, :, N], ALU.subtract).then_inc(sem("pool_d"), 1)

            for layer in range(2):
                xw, a_b = sem(f"moe{layer}_xw"), sem(f"moe{layer}_b")
                pool.wait_ge(sem("moe_xst"), 16 * layer + 16)
                pool.wait_ge(sem("moe_tail"), layer + 1)
                pool.wait_ge(sem("moe_plan"), layer + 1)
                n = pool.value_load(plan[0:1, 1:2], min_val=EXPERTS // 2, max_val=MAX_ROUNDS * EXPERTS // 2)

                def window(e, s):
                    at = pool.value_load(STI[0:1, bass.ds(e, 1)] if not isinstance(e, int) else STI[0:1, e:e + 1],
                                         min_val=0, max_val=PAIRS)
                    pool.tensor_copy(XW[:, s], XST[:, :, bass.ds(at, WIN)]).then_inc(xw, 1)

                for s in range(2):
                    window(s, s)
                with pool.Fori(1, n) as i:
                    for s in range(2):
                        pool.wait_ge(a_b, i * 2 + (s - 1))
                        window(i * 2 + s, s)
                if layer == 0:
                    pool.wait_ge(sem("h"), 40)
                    pool.dma_start(BKT[0:BUCKETS], A["consts"][0:BUCKETS, CC["bucket"]:CC["bucket"] + 640])\
                        .then_inc(sem("bkt"), 16)
                    pool.dma_start(RB[0:BUCKETS], A["rel_bias"]).then_inc(sem("bkt"), 16)
                    pool.wait_ge(sem("vb"), 2)
                    pool.dma_start(scratch, VB[0:HEADS2]).then_inc(sem("vb_out"), 16)
                    pool.wait_ge(sem("vb_out"), 16)
                    pool.dma_start(spread, scratch.partition_broadcast(P)).then_inc(sem("spread"), 16)
                    pool.wait_ge(sem("spread"), 16)
                    shifted = bass.AP(spread.tensor, P - 1, [[HEADS2 * 640 - 1, P], [640, HEADS2], [1, SEQ]])
                    pool.dma_start(TOE, shifted).then_inc(sem("toe"), 16)

        @block.scalar
        def _(act):
            st = Steps(act, sem("act_step"))
            A_ = nc.scalar.activation
            act.dma_start(xtok, A["x"].rearrange("a (t p) d -> p (a t) d", p=P)).then_inc(sem("x_in"), 16)
            act.dma_start(keep[:], A["consts"][:, 0:N_KEEP]).then_inc(sem("keep"), 16)
            act.dma_start(par[:], A["params"]).then_inc(sem("par"), 16)

            def evac(dst, src, s):
                A_(dst, src, ACT.Copy).then_inc(sem(s), 1)

            act.wait_ge(sem("par"), 16)
            A_(csil[:], par[:, PC["c"]:PC["c"] + KT], ACT.Silu).then_inc(sem("csil"), 1)
            for k in range(KT):
                act.wait_ge(sem("x_tp"), k + 1)
                evac(H[:, k], bank[k % 4][:], "x_h")

            def norm(i, ln, shift):
                for k in range(KT):
                    if ln:
                        act.wait_ge(sem("centred"), 8 * (ln - 1) + k + 1)
                    elif k == 0:
                        act.wait_ge(sem("x_h") if i == 0 else sem("h"), 8 if i == 0 else 8 * i)
                    A_(U[:, k], H[:, k], ACT.Square).then_inc(sem("squares"), 1)
                if i == 0:
                    act.wait_ge(sem("eps"), 3)
                act.wait_ge(sem("sumsq"), i + 1)
                if i:
                    act.wait_ge(sem("normed"), 8 * i)
                A_(rstd[:], bank[7][:], ACT.Sqrt, scale=1.0 / D,
                   bias=epsc[:, 1:2] if ln else epsc[:, 0:1]).then_inc(sem("root"), 1)
                for k in range(KT):
                    act.wait_ge(sem("normed"), 8 * i + k + 1)
                    A_(U[:, k], U[:, k], ACT.Identity, bias=shift(k)).then_inc(sem("u"), 1)

            def ffn(i):
                a, silu, base = sem("ffn_a"), sem("ffn_silu"), FT * i
                body = 6

                def tile(j, r):
                    act.wait_ge(a, j + (base + 1))
                    dst = G[:, j] if isinstance(j, int) else G[:, bass.ds(j, 1)].rearrange("p a s -> p (a s)")
                    A_(dst, bank[2 * (r % 2)][:], ACT.Silu).then_inc(silu, 1)

                for j in range(2):
                    tile(j, j)
                with act.Fori(0, 3) as it:
                    for r in range(body):
                        tile(it * body + (2 + r), r)
                for j in range(20, 22):
                    tile(j, j)

            def to_tokens(n):
                if n < 2:
                    act.wait_ge(sem("h"), 32 + 16 * n)
                for g in range(8):
                    act.wait_ge(sem("xt_tp"), 8 * n + g + 1)
                    t, half = g // 2, g % 2
                    evac(XT[:, t, 512 * half:512 * half + 512], bank[g % 4][:], "xt")

            def moe(l):
                to_tokens(l)
                act.wait_ge(sem("moe_m"), l + 1)
                for t in range(TT):
                    A_(RK[:, 96 + 8 * t:104 + 8 * t], LG[:, t, 0:GROUPS], ACT.Exp, bias=RK[:, 64 + t:65 + t],
                       accum_out=RK[:, 68 + t:69 + t]).then_inc(sem("moe_ge"), 1)
                act.wait_ge(sem("moe_d"), l + 1)
                A_(RK[:, 76:80], RK[:, 72:76], ACT.Exp).then_inc(sem("moe_ee"), 1)
                for g in range(16):
                    act.wait_ge(sem("moe_gather"), 16 * l + g + 1)
                    c, k = g // 8, g % 8
                    evac(XST[:, k, 512 * c:512 * c + 512], bank[g % 4][:], "moe_xst")
                act.wait_ge(sem("moe_plan"), l + 1)
                n = act.value_load(plan[0:1, 1:2], min_val=EXPERTS // 2, max_val=MAX_ROUNDS * EXPERTS // 2)
                with act.Fori(0, n) as i:
                    for s in range(2):
                        act.wait_ge(sem(f"moe{l}_a"), i * 2 + s + 1)
                        act.wait_ge(sem(f"moe{l}_h"), i * 2)
                        A_(SA[:, s], bank[s][:, 0:2 * WIN], ACT.Silu).then_inc(sem(f"moe{l}_silu"), 1)
                for g in range(16):
                    act.wait_ge(sem("moe_ystp"), 16 * l + g + 1)
                    evac(YS[:, g // 2, 512 * (g % 2):512 * (g % 2) + 512], bank[g % 4][:], "moe_ys")

            norm(0, 0, lambda k: mod[:, k:k + 1])
            ffn(0)
            norm(1, 0, lambda k: mod[:, 24 + k:25 + k])
            act.wait_ge(sem("angles"), 1)
            A_(sinT, TB[:, 2], ACT.Sin).then_inc(sem("tables"), 1)
            A_(cosT, TB[:, 4], ACT.Sin).then_inc(sem("tables"), 1)
            for m in range(42):
                act.wait_ge(sem("mix_tile"), m + 1)
                src = bank[m % 4][:]
                if m < 2:
                    evac(PB[:, m, 16:528], src, "mix_evac")
                elif m < 8:
                    act.wait_ge(sem("tables"), 2)
                    evac(Q[:, m - 2], src, "mix_evac")
                elif m < 14:
                    evac(K[:, m - 8], src, "mix_evac")
                elif m < 26:
                    evac(V[:, (m - 14) // 4, (m - 14) % 4], src[:, 0:256], "mix_evac")
                else:
                    A_(GT[:, m - 26], src, ACT.Sigmoid).then_inc(sem("mix_evac"), 1)
            for k in range(2):
                act.wait_ge(sem("yp_mm"), k + 1)
                A_(YP[:, k], bank[6 + k][:], ACT.Copy, scale=col("pool_scale", k)).then_inc(sem("yp"), 1)

            def att_out(u):
                h, c = u // CLASSES, u % CLASSES
                act.wait_ge(sem("att_tp"), u + 1)
                if u:
                    act.wait_ge(sem("att_pv"), u)
                st.did(A_(PT1[:, 0:4].rearrange("p a b -> p (a b)"), bank[4][:], ACT.Copy))
                A_(PT1[:, 4:6].rearrange("p a b -> p (a b)"), bank[5][:, 0:256], ACT.Copy).then_inc(sem("att_pt"), 1)

            def att_y(u):
                h, c = u // CLASSES, u % CLASSES
                r = 64 * (h % 2)
                act.wait_ge(sem("att_pv"), u + 1)
                evac(YA[r:r + 64, h // 2, c:SEQ:CLASSES], bank[6 + u % 2][r:r + 64, 0:P], "att_y")

            for u in range(16):
                act.wait_ge(sem("att_max"), u + 1)
                A_(S1[:, u % 2], S1[:, u % 2], ACT.Exp, bias=small[:, u:u + 1],
                   accum_out=small[:, 16 + u:17 + u]).then_inc(sem("att_e"), 1)
                if u:
                    att_out(u - 1)
                act.wait_ge(sem("att_ri"), u + 1)
                A_(S1[:, u % 2], S1[:, u % 2], ACT.Copy, scale=small[:, 32 + u:33 + u]).then_inc(sem("att_p"), 1)
                if u:
                    att_y(u - 1)
            att_out(15)
            att_y(15)
            norm(2, 0, lambda k: mod[:, 48 + k:49 + k])
            ffn(1)
            norm(3, 0, lambda k: epsc[:, 2:3])
            for d in range(KT):
                act.wait_ge(sem("conv_c"), d + 1)
                if d >= 2:
                    act.wait_ge(sem("conv_u"), d - 1)
                evac(CG[:, d % 2], bank[3 * (d % 2)][:], "conv_cg")
            norm(4, 1, lambda k: col("ln1_b", k))
            moe(0)
            norm(5, 2, lambda k: col("ln2_b", k))
            for t in range(4):
                act.wait_ge(sem("qi_mm"), t + 1)
                evac(QI[:, t], bank[t][:], "qi")
            act.wait_ge(sem("var"), 1)
            A_(DS[:, 216:224], DS[:, 192:200], ACT.Sqrt).then_inc(sem("sdev"), 1)
            act.wait_ge(sem("kv_tp"), 1)
            evac(CKVT, bank[6][:], "kvt")
            act.wait_ge(sem("kv_tp"), 2)
            evac(KIT, bank[7][:], "kvt")
            m = 0
            for qb in range(1, TT):
                for h in range(IDX_HEADS):
                    act.wait_ge(sem("idx_mm"), m + 1)
                    if m >= 2:
                        act.wait_ge(sem("idx_acc"), m - 1)
                    A_(IR[:, m % 2, 0:(qb + 1) * P], bank[m % 4][:, 0:(qb + 1) * P], ACT.Relu,
                       scale=IDX_DIM ** -0.5).then_inc(sem("idx_relu"), 1)
                    m += 1
            for h in range(HEADS2):
                act.wait_ge(sem("dsa_q"), h + 1)
                evac(Q2[:, h], bank[4 + h % 4][:], "q2")
            units = [(qb, h) for qb in range(TT) for h in range(HEADS2)]

            def turn(u):
                qb, h = units[u]
                n = (qb + 1) * P
                act.wait_ge(sem("ds_tp"), u + 1)
                if u >= 2:
                    act.wait_ge(sem("ds_pv"), u - 1)
                A_(PT2[:, u % 2, 0:n], bank[2 + u % 2][:, 0:n], ACT.Copy).then_inc(sem("ds_pt"), 1)

            for u, (qb, h) in enumerate(units):
                n = (qb + 1) * P
                act.wait_ge(sem("ds_max"), u + 1)
                A_(S2[:, u % 2, 0:n], S2[:, u % 2, 0:n], ACT.Exp, bias=DS[:, u:u + 1],
                   accum_out=DS[:, 64 + u:65 + u]).then_inc(sem("ds_e"), 1)
                if u:
                    turn(u - 1)
                act.wait_ge(sem("ds_ri"), u + 1)
                A_(S2[:, u % 2, 0:n], S2[:, u % 2, 0:n], ACT.Copy, scale=DS[:, 128 + u:129 + u])\
                    .then_inc(sem("ds_p"), 1)
            turn(len(units) - 1)
            norm(6, 3, lambda k: col("ln1_b", 8 + k))
            moe(1)
            norm(7, 4, lambda k: col("ln2_b", 8 + k))
            to_tokens(2)

        @block.vector
        def _(dve):
            st = Steps(dve, sem("dve_step"))
            TSc, STT, TTn = nc.vector.tensor_scalar, nc.vector.scalar_tensor_tensor, nc.vector.tensor_tensor

            def seq(ins):
                st.did(ins)
                st.wait()

            dve.wait_ge(sem("par"), 16)
            dve.wait_ge(sem("ada_used"), 36)
            seq(TTn(mod[:], bank[4][:, 0:72], par[:, PC["b_ada"]:PC["b_ada"] + 72], ALU.add))
            for i, g in enumerate(("g_ffn1", "g_mix", "g_ffn2")):
                a = 24 * i
                st.did(STT(out=gains[:, 8 * i:8 * i + 8], in0=mod[:, a + 8:a + 16], scalar=1.0,
                           in1=par[:, PC[g]:PC[g] + 8], op0=ALU.add, op1=ALU.mult))
                st.did(TSc(gates[:, 8 * i:8 * i + 8], mod[:, a + 16:a + 24], (0.5, 1.0, 0.5)[i], None, ALU.mult))
            st.wait()

            def norm(i, ln, gain):
                if ln:
                    dve.wait_ge(sem("mean"), ln)
                    for k in range(KT):
                        STT(out=H[:, k], in0=bank[6][:], scalar=-1.0 / D, in1=H[:, k],
                            op0=ALU.mult, op1=ALU.add).then_inc(sem("centred"), 1)
                dve.wait_ge(sem("root"), i + 1)
                seq(nc.vector.reciprocal(rstd[:], rstd[:]))
                for k in range(KT):
                    STT(out=U[:, k], in0=H[:, k], scalar=gain(k), in1=rstd[:],
                        op0=ALU.mult, op1=ALU.mult).then_inc(sem("normed"), 1)

            def ffn(i):
                b, g, silu, base = sem("ffn_b"), sem("ffn_g"), sem("ffn_silu"), FT * i

                def tile(j, r):
                    dve.wait_ge(silu, j + (base + 1))
                    dve.wait_ge(b, j + (base + 1))
                    dst = G[:, j] if isinstance(j, int) else G[:, bass.ds(j, 1)].rearrange("p a s -> p (a s)")
                    TTn(dst, bank[2 * (r % 2) + 1][:], dst, ALU.mult).then_inc(g, 1)

                for j in range(2):
                    tile(j, j)
                with dve.Fori(0, 3) as it:
                    for r in range(6):
                        tile(it * 6 + (2 + r), r)
                for j in range(20, 22):
                    tile(j, j)

            def gated_add(name, n, gate):
                for half in range(2):
                    dve.wait_ge(sem(name + "_used"), n * (half + 1))
                    for d in range(4):
                        k = 4 * half + d
                        STT(out=H[:, k], in0=bank[k][:], scalar=gates[:, gate + k:gate + k + 1], in1=H[:, k],
                            op0=ALU.mult, op1=ALU.add).then_inc(sem("h"), 1)

            def deep_add(k, src):
                STT(out=H[:, k], in0=U[:, k], scalar=ALPHA, in1=src, op0=ALU.mult, op1=ALU.add)\
                    .then_inc(sem("h"), 1)

            norm(0, 0, lambda k: gains[:, k:k + 1])
            ffn(0)
            gated_add("ffn0_out", 6, 0)
            dve.wait_ge(sem("mix_const"), 80)
            ang, k1, r1, r2 = TB[:, 0], TB[:, 1], TB[:, 2], TB[:, 4]
            big = 12582912.0
            seq(nc.vector.tensor_copy(ang, posi))
            seq(TSc(ang, ang, invf[:, 0:1], None, ALU.mult))
            seq(TSc(k1, ang, 1.0 / (2 * np.pi), big, ALU.mult, ALU.add))
            seq(TSc(k1, k1, big, None, ALU.subtract))
            c1 = 6.28125
            c2 = float(np.float32(np.round((2 * np.pi - c1) * 2 ** 22) / 2 ** 22))
            c3 = float(2 * np.pi - c1 - c2)
            seq(STT(out=r1, in0=k1, scalar=-c1, in1=ang, op0=ALU.mult, op1=ALU.add))
            seq(STT(out=r1, in0=k1, scalar=-c2, in1=r1, op0=ALU.mult, op1=ALU.add))
            seq(STT(out=r1, in0=k1, scalar=-c3, in1=r1, op0=ALU.mult, op1=ALU.add))
            top = 3.1415925
            seq(TSc(r2, r1, float(np.pi / 2), None, ALU.add))
            seq(TSc(TB[:, 3], r2, float(np.pi), float(-2 * np.pi), ALU.is_gt, ALU.mult))
            seq(TTn(r2, r2, TB[:, 3], ALU.add))
            seq(TSc(r2, r2, top, -top, ALU.min, ALU.max))
            TSc(r1, r1, top, -top, ALU.min, ALU.max).then_inc(sem("angles"), 1)
            norm(1, 0, lambda k: gains[:, 8 + k:9 + k])
            dve.wait_ge(sem("tables"), 2)
            for r in range(12):
                t = Q[:, r] if r < 6 else K[:, r - 6]
                dve.wait_ge(sem("rot"), r + 1)
                st.did(TTn(RT[:, 0], t, cosT, ALU.mult))
                st.did(TTn(RT[:, 1], bank[4 + r % 2][:], sinT, ALU.mult))
                st.wait()
                TTn(t, RT[:, 0], RT[:, 1], ALU.add).then_inc(sem("rope"), 1)
                dve.wait_ge(sem("rope"), r + 1)
            dve.wait_ge(sem("pool_d"), 1)
            dve.wait_ge(sem("yp"), 2)
            for u in range(16):
                c = u % CLASSES
                lo, hi = bank[2 * (u % 2)], bank[2 * (u % 2) + 1]
                dve.wait_ge(sem("att_mm"), u + 1)
                if u >= 2:
                    dve.wait_ge(sem("att_tp"), u - 1)
                st.did(STT(out=S1[:, u % 2, 0:512], in0=lo[:], scalar=HEAD ** -0.5, in1=band[:, c],
                           op0=ALU.mult, op1=ALU.add))
                st.did(STT(out=S1[:, u % 2, 512:640], in0=hi[:, 0:P], scalar=HEAD ** -0.5, in1=causal,
                           op0=ALU.mult, op1=ALU.add))
                STT(out=S1[:, u % 2, 640:768], in0=hi[:, P:2 * P], scalar=HEAD ** -0.5, in1=mod4,
                    op0=ALU.mult, op1=ALU.add).then_inc(sem("att_s"), 1)
                st.wait()
                dve.wait_ge(sem("att_s"), u + 1)
                nc.vector.tensor_reduce(small[:, u:u + 1], S1[:, u % 2], AXX, ALU.max, negate=True)\
                    .then_inc(sem("att_max"), 1)
                dve.wait_ge(sem("att_e"), u + 1)
                nc.vector.reciprocal(small[:, 32 + u:33 + u], small[:, 16 + u:17 + u]).then_inc(sem("att_ri"), 1)
            dve.wait_ge(sem("att_y"), 16)
            for d in range(KT):
                dve.wait_ge(sem("merge_ab"), d + 1)
                st.did(TTn(MG[:, d], bank[(2 * d) % 4][:], GT[:, d], ALU.mult))
                st.did(TTn(RT2[:], bank[(2 * d + 1) % 4][:], GT[:, 8 + d], ALU.mult))
                st.wait()
                TTn(MG[:, d], MG[:, d], RT2[:], ALU.add).then_inc(sem("merged"), 1)
                dve.wait_ge(sem("merged"), d + 1)
            gated_add("mix_out", 2, 8)
            norm(2, 0, lambda k: gains[:, 16 + k:17 + k])
            ffn(1)
            gated_add("ffn1_out", 6, 16)
            norm(3, 0, lambda k: col("g_final", k))
            st.did(nc.vector.memset(CU[:, :, 0:2], 0.0))
            st.wait()
            for d in range(KT):
                b3 = 3 * (d % 2)
                cu, cv = CU[:, d % 2], CV[:, d % 2]
                dve.wait_ge(sem("conv_cg"), d + 1)
                dve.wait_ge(sem("conv_h"), d + 1)
                TTn(cu[:, 2:SEQ + 2], bank[b3 + 1][:], CG[:, d % 2], ALU.mult).then_inc(sem("conv_u"), 1)
                dve.wait_ge(sem("conv_u"), d + 1)
                seq(TSc(cv, cu[:, 0:SEQ], col("conv_k", d), None, ALU.mult))
                seq(STT(out=cv, in0=cu[:, 1:SEQ + 1], scalar=col("conv_k", 8 + d), in1=cv, op0=ALU.mult, op1=ALU.add))
                seq(STT(out=cv, in0=cu[:, 2:SEQ + 2], scalar=col("conv_k", 16 + d), in1=cv, op0=ALU.mult, op1=ALU.add))
                dve.wait_ge(sem("conv_b"), d + 1)
                TTn(BC[:, d], bank[b3 + 2][:], cv, ALU.mult).then_inc(sem("conv_bc"), 1)

            def deep_out(name, n):
                for half in range(2):
                    dve.wait_ge(sem(name + "_used"), n * (half + 1))
                    for d in range(4):
                        deep_add(4 * half + d, bank[4 * half + d][:])

            deep_out("conv_out", 2)
            norm(4, 1, lambda k: col("ln1_g", k))

            def moe(l):
                dve.wait_ge(sem("rows"), 16 * 11)
                T4 = range(TT)
                r = RK
                top, idx = r[:, 0:32], r[:, 32:64].bitcast(U32)
                negm, gden, dif, ex = r[:, 64:68], r[:, 68:72], r[:, 72:76], r[:, 76:80]
                gi, w0, w1, id0, id1 = r[:, 80:84], r[:, 84:88], r[:, 88:92], r[:, 92:96], r[:, 128:132]
                d0, d1 = r[:, 132:136], r[:, 136:140]
                cnt, cum, one64 = r[:, 144:208], r[:, 208:272], r[:, 272:336]
                el, oh = r[:, 336:368], r[:, 368:400]
                etop, eidx = r[:, 400:432], r[:, 432:464].bitcast(U32)
                E0, E1, EA, RN = r[:, 512:768], r[:, 768:1024], r[:, 1024:1280], r[:, 1280:1536]
                tmp = r[:, 1536:1792]
                cell = lambda v, t, n: v[:, n * t:n * t + n]
                dve.wait_ge(sem("moe_logits"), l + 1)
                for t in T4:
                    st.did(TTn(LG[:, t], bank[4][:, 72 * t:72 * t + 72], rbias[:, l], ALU.add))
                st.wait()
                for t in T4:
                    st.did(nc.vector.max(cell(top, t, 8), LG[:, t, 0:GROUPS]))
                st.wait()
                for t in T4:
                    st.did(TSc(cell(negm, t, 1), top[:, 8 * t:8 * t + 1], -1.0, None, ALU.mult))
                    st.did(nc.vector.max_index(cell(idx, t, 8), cell(top, t, 8), LG[:, t, 0:GROUPS]))
                st.wait()
                for t in T4:
                    i = nc.vector.tensor_copy(cell(gi, t, 1), idx[:, 8 * t:8 * t + 1])
                    i.then_inc(sem("moe_m"), 1) if t == TT - 1 else st.did(i)
                st.wait()
                dve.wait_ge(sem("moe_m"), l + 1)
                for t in T4:
                    st.did(TSc(cell(oh, t, 8), lane[:, 0:8], cell(gi, t, 1), None, ALU.is_equal))
                st.wait()
                for g in range(GROUPS):
                    for t in T4:
                        src = LG[:, t, 8 + 8 * g:16 + 8 * g]
                        o = oh[:, 8 * t + g:8 * t + g + 1]
                        if g == 0:
                            st.did(TSc(cell(el, t, 8), src, o, None, ALU.mult))
                        else:
                            st.did(STT(out=cell(el, t, 8), in0=src, scalar=o, in1=cell(el, t, 8),
                                       op0=ALU.mult, op1=ALU.add))
                    st.wait()
                for t in T4:
                    st.did(nc.vector.max(cell(etop, t, 8), cell(el, t, 8)))
                st.wait()
                for t in T4:
                    st.did(nc.vector.max_index(cell(eidx, t, 8), cell(etop, t, 8), cell(el, t, 8)))
                    i = TTn(cell(dif, t, 1), etop[:, 8 * t + 1:8 * t + 2], etop[:, 8 * t:8 * t + 1], ALU.subtract)
                    i.then_inc(sem("moe_d"), 1) if t == TT - 1 else st.did(i)
                st.wait()
                for t in T4:
                    st.did(nc.vector.tensor_copy(cell(id0, t, 1), eidx[:, 8 * t:8 * t + 1]))
                    st.did(nc.vector.tensor_copy(cell(id1, t, 1), eidx[:, 8 * t + 1:8 * t + 2]))
                st.wait()
                for i in (id0, id1):
                    st.did(STT(out=i, in0=gi, scalar=float(PER_GROUP), in1=i, op0=ALU.mult, op1=ALU.add))
                st.wait()
                for t in T4:
                    st.did(TSc(cell(E0, t, 64), lane[:, 0:64], cell(id0, t, 1), None, ALU.is_equal))
                    st.did(TSc(cell(E1, t, 64), lane[:, 0:64], cell(id1, t, 1), None, ALU.is_equal))
                st.wait()
                TTn(EA, E0, E1, ALU.add).then_inc(sem("moe_ea"), 1)
                dve.wait_ge(sem("moe_ge"), 4 * l + 4)
                dve.wait_ge(sem("moe_ee"), l + 1)
                seq(STT(out=w0, in0=ex, scalar=1.0, in1=gden, op0=ALU.add, op1=ALU.mult))
                seq(nc.vector.reciprocal(w0, w0))
                st.did(TTn(w1, w0, ex, ALU.mult))
                dve.wait_ge(sem("moe_rank"), l + 1)
                st.did(nc.vector.tensor_copy(cnt, bank[5][:, 256:320]))
                st.did(nc.vector.memset(one64, 1.0))
                st.wait()
                seq(nc.vector.tensor_tensor_scan(cum, one64, cnt, 0.0, ALU.mult, ALU.add))
                seq(TTn(startf, cum, cnt, ALU.subtract))
                for t in T4:
                    st.did(TTn(cell(RN, t, 64), bank[5][:, 64 * t:64 * t + 64], startf, ALU.add))
                st.wait()
                for t in T4:
                    for E, d in ((E0, d0), (E1, d1)):
                        seq(nc.vector.tensor_tensor_reduce(tmp[:, 0:64], cell(E, t, 64), cell(RN, t, 64), 1.0, 0.0,
                                                           ALU.mult, ALU.add, cell(d, t, 1)))
                for j in range(MAX_ROUNDS):
                    st.did(TSc(REM[:, 64 * j:64 * j + 64], cnt, float(WIN * j), None, ALU.subtract))
                    st.did(TSc(STI[:, 64 * j:64 * j + 64], startf, float(WIN * j), float(PAIRS), ALU.add, ALU.min))
                seq(nc.vector.tensor_reduce(tmp[:, 0:1], cnt, AXX, ALU.max))
                seq(TSc(plan[:, 2:3], tmp[:, 0:1], float(WIN - 1), None, ALU.add))
                seq(TSc(plan[:, 0:1], plan[:, 2:3], 6, None, ALU.arith_shift_right))
                st.did(TSc(plan[:, 3:4], plan[:, 0:1], 6, None, ALU.logical_shift_left))
                st.wait()
                seq(TSc(plan[:, 2:3], plan[:, 3:4], 1.0, None, ALU.subtract))
                TSc(plan[:, 1:2], plan[:, 0:1], 5, None, ALU.logical_shift_left).then_inc(sem("moe_plan"), 1)
                for t in T4:
                    seq(TSc(SELW[:, t], slotrow, cell(d0, t, 1), None, ALU.is_equal))
                    STT(out=SEL[:, t], in0=slotrow, scalar=cell(d1, t, 1), in1=SELW[:, t],
                        op0=ALU.is_equal, op1=ALU.add).then_inc(sem("moe_sel"), 1)
                for t in T4:
                    dve.wait_ge(sem("moe_sel"), 4 * l + t + 1)
                nc.vector.memset(XST[:, :, PAIRS:SLOTS], 0.0).then_inc(sem("moe_tail"), 1)
                for t in T4:
                    seq(TSc(SELT, slotrow, cell(d1, t, 1), cell(w1, t, 1), ALU.is_equal, ALU.mult))
                    seq(STT(out=SELW[:, t], in0=SELW[:, t], scalar=cell(w0, t, 1), in1=SELT,
                            op0=ALU.mult, op1=ALU.add))
                dve.wait_ge(sem("moe_gather"), 16 * l + 16)
                nc.vector.memset(YST, 0.0).then_inc(sem(f"moe{l}_add"), 1)
                dve.wait_ge(sem("moe_plan"), l + 1)
                n = dve.value_load(plan[0:1, 1:2], min_val=EXPERTS // 2, max_val=MAX_ROUNDS * EXPERTS // 2)
                with dve.Fori(0, n) as i:
                    for s in range(2):
                        e = i * 2 + s
                        at = dve.value_load(STI[0:1, bass.ds(e, 1)], min_val=0, max_val=PAIRS)
                        dve.wait_ge(sem(f"moe{l}_silu"), e + 1)
                        dve.wait_ge(sem(f"moe{l}_b"), e + 1)
                        TTn(HB[:, s], bank[2 + s][:, 0:2 * WIN], SA[:, s], ALU.mult).then_inc(sem(f"moe{l}_hb"), 1)
                        dve.wait_ge(sem(f"moe{l}_hb"), e + 1)
                        STT(out=HM[:, s], in0=lane, scalar=REM[:, bass.ds(e, 1)], in1=HB[:, s],
                            op0=ALU.is_lt, op1=ALU.mult).then_inc(sem(f"moe{l}_h"), 1)
                        dve.wait_ge(sem(f"moe{l}_y"), e + 1)
                        dve.wait_ge(sem(f"moe{l}_add"), e + 1)
                        w = YST[:, :, bass.ds(at, WIN)]
                        TTn(w, bank[4 + s][:].rearrange("p (k n) -> p k n", k=KT), w, ALU.add)\
                            .then_inc(sem(f"moe{l}_add"), 1)
                for g in range(8):
                    dve.wait_ge(sem("moe_swtp"), 8 * l + g + 1)
                    nc.vector.tensor_copy(SWT[:, g], bank[4 + g % 4][:]).then_inc(sem("moe_swt"), 1)
                for d in range(KT):
                    dve.wait_ge(sem("moe_f"), 8 * l + d + 1)
                    deep_add(d, bank[d % 4][:])

            moe(0)
            norm(5, 2, lambda k: col("ln2_g", k))

            dve.wait_ge(sem("vb_mm"), 1)
            nc.vector.tensor_copy(VB[0:HEADS2, 0:512], bank[6][0:HEADS2, :]).then_inc(sem("vb"), 1)
            nc.vector.tensor_copy(VB[0:HEADS2, 512:640], bank[7][0:HEADS2, 0:P]).then_inc(sem("vb"), 1)
            dve.wait_ge(sem("kv_mm"), 1)
            sq = S2
            for t in range(TT):
                src = bank[4][:, P * t:P * t + P]
                st.did(nc.vector.tensor_copy(CKV[:, t], src))
            st.wait()
            for t in range(TT):
                seq(nc.vector.tensor_tensor_reduce(S2[:, 0, 0:P], CKV[:, t], CKV[:, t], 1.0, 0.0,
                                                   ALU.mult, ALU.add, DS[:, 192 + t:193 + t]))
            seq(TSc(DS[:, 192:196], DS[:, 192:196], 1.0 / LATENT, RMS_EPS, ALU.mult, ALU.add))
            dve.wait_ge(sem("ki_mm"), 1)
            for t in range(TT):
                st.did(nc.vector.tensor_copy(KI[:, t, 0:64], bank[5][:, 72 * t:72 * t + 64]))
                st.did(TSc(W8[:, t], bank[5][:, 72 * t + 64:72 * t + 72], IDX_HEADS ** -0.5, None, ALU.mult))
            st.wait()
            for t in range(TT):
                st.did(nc.vector.tensor_reduce(DS[:, 200 + t:201 + t], KI[:, t, 0:64], AXX, ALU.add))
            st.wait()
            seq(TSc(DS[:, 200:204], DS[:, 200:204], 1.0 / IDX_DIM, None, ALU.mult))
            for t in range(TT):
                st.did(TSc(KI[:, t, 0:64], KI[:, t, 0:64], DS[:, 200 + t:201 + t], None, ALU.subtract))
            st.wait()
            for t in range(TT):
                seq(nc.vector.tensor_tensor_reduce(S2[:, 0, 0:64], KI[:, t, 0:64], KI[:, t, 0:64], 1.0, 0.0,
                                                   ALU.mult, ALU.add, DS[:, 196 + t:197 + t]))
            seq(TSc(DS[:, 196:200], DS[:, 196:200], 1.0 / IDX_DIM, LN_EPS, ALU.mult, ALU.add))
            nc.vector.tensor_copy(DS[:, 204:205], DS[:, 196:197]).then_inc(sem("var"), 1)
            dve.wait_ge(sem("sdev"), 1)
            seq(nc.vector.reciprocal(DS[:, 208:216], DS[:, 216:224]))
            for t in range(TT):
                STT(out=CKV[:, t], in0=CKV[:, t], scalar=DS[:, 208 + t:209 + t], in1=kvg[:],
                    op0=ALU.mult, op1=ALU.mult).then_inc(sem("ckv"), 1)
            for t in range(TT):
                st.did(STT(out=KI[:, t, 0:64], in0=KI[:, t, 0:64], scalar=DS[:, 212 + t:213 + t], in1=lng[:],
                           op0=ALU.mult, op1=ALU.mult))
            st.wait()
            for t in range(TT):
                st.did(TTn(KI[:, t, 64:128], KI[:, t, 0:64], lnb[:], ALU.add))
            st.wait()
            for t in range(TT):
                nc.vector.tensor_copy(KI[:, t, 0:64], KI[:, t, 64:128]).then_inc(sem("ki"), 1)
            m = 0
            for qb in range(1, TT):
                n = (qb + 1) * P
                acc = SM[:, qb - 1, 0:n]
                for h in range(IDX_HEADS):
                    dve.wait_ge(sem("idx_relu"), m + 1)
                    w = W8[:, qb, h:h + 1]
                    if h == 0:
                        TSc(acc, IR[:, m % 2, 0:n], w, None, ALU.mult).then_inc(sem("idx_acc"), 1)
                    else:
                        STT(out=acc, in0=IR[:, m % 2, 0:n], scalar=w, in1=acc, op0=ALU.mult, op1=ALU.add)\
                            .then_inc(sem("idx_acc"), 1)
                    m += 1
                    dve.wait_ge(sem("idx_acc"), m)
                st.did(TTn(acc[:, n - P:n], acc[:, n - P:n], causal, ALU.add))
            st.wait()
            for r in range(TOPK // 8):
                for qb in range(1, TT):
                    acc = SM[:, qb - 1, 0:(qb + 1) * P]
                    st.did(nc.vector.max(DS[:, 224 + 8 * qb:232 + 8 * qb], acc))
                st.wait()
                for qb in range(1, TT):
                    acc = SM[:, qb - 1, 0:(qb + 1) * P]
                    st.did(nc.vector.match_replace(acc, DS[:, 224 + 8 * qb:232 + 8 * qb], acc, TAKEN))
                st.wait()
            for qb in range(1, TT):
                acc = SM[:, qb - 1, 0:(qb + 1) * P]
                st.did(TSc(acc, acc, TAKEN / 2, NEG, ALU.is_gt, ALU.mult))
            st.wait()
            units = [(qb, h) for qb in range(TT) for h in range(HEADS2)]
            dve.wait_ge(sem("toe"), 16)

            def out_of(u):
                qb, h = units[u]
                dve.wait_ge(sem("ds_pv"), u + 1)
                nc.vector.tensor_copy(Q2[:, h, qb * P:qb * P + P], bank[4 + u % 2][:, 0:P]).then_inc(sem("ds_o"), 1)

            for u, (qb, h) in enumerate(units):
                n = (qb + 1) * P
                S = S2[:, u % 2, 0:n]
                dve.wait_ge(sem("ds_mm"), u + 1)
                if u >= 2:
                    dve.wait_ge(sem("ds_tp"), u - 1)
                STT(out=S, in0=bank[u % 2][:, 0:n], scalar=LATENT ** -0.5, in1=TOE[:, h, SEQ - n:SEQ],
                    op0=ALU.mult, op1=ALU.add).then_inc(sem("ds_s"), 1)
                dve.wait_ge(sem("ds_s"), u + 1)
                if qb == 0:
                    seq(TTn(S, S, causal, ALU.add))
                else:
                    seq(TTn(S, S, SM[:, qb - 1, 0:n], ALU.add))
                nc.vector.tensor_reduce(DS[:, u:u + 1], S, AXX, ALU.max, negate=True).then_inc(sem("ds_max"), 1)
                if u >= 2:
                    out_of(u - 2)
                dve.wait_ge(sem("ds_e"), u + 1)
                nc.vector.reciprocal(DS[:, 128 + u:129 + u], DS[:, 64 + u:65 + u]).then_inc(sem("ds_ri"), 1)
            out_of(62)
            out_of(63)
            deep_out("dsa_out", 4)
            norm(6, 3, lambda k: col("ln1_g", 8 + k))
            moe(1)
            norm(7, 4, lambda k: col("ln2_g", 8 + k))

        @block.tensor
        def _(pe):
            mm, tp = nc.tensor.matmul, nc.tensor.transpose
            pe.wait_ge(sem("x_in"), 16)
            pe.wait_ge(sem("keep"), 16)
            for k in range(KT):
                if k >= 4:
                    pe.wait_ge(sem("x_h"), k - 3)
                for t in range(TT):
                    i = tp(bank[k % 4][:, P * t:P * t + P], xtok[:, t, P * k:P * k + P], ident)
                i.then_inc(sem("x_tp"), 1)
            pe.wait_ge(sem("csil"), 1)
            with pe.Fori(0, 6) as it:
                for c in range(6):
                    landed(pe, "a", c, it * 16)
                    for j in range(2):
                        for k in range(KT):
                            i = mm(bank[4][:, bass.ds(it * 12 + (2 * c + j), 1)], chunk("a", c)[:, k, P * j:P * j + P],
                                   csil[:, k:k + 1], start=(k == 0), stop=(k == KT - 1))
                    i.then_inc(sem("ada_used"), 1)

            def norm(i, ln):
                if i == 0:
                    pe.wait_ge(sem("pool_step"), 1)
                if ln:
                    pe.wait_ge(sem("h"), 8 * (i))
                    for k in range(KT):
                        x = mm(bank[6][:], ones[:], H[:, k], start=(k == 0), stop=(k == KT - 1))
                    x.then_inc(sem("mean"), 1)
                for k in range(KT):
                    pe.wait_ge(sem("squares"), 8 * i + k + 1)
                    x = mm(bank[7][:], ones[:], U[:, k], start=(k == 0), stop=(k == KT - 1))
                x.then_inc(sem("sumsq"), 1)

            def ffn(i):
                n0 = first[f"ffn{i}"]
                a, b, g, base = sem("ffn_a"), sem("ffn_b"), sem("ffn_g"), FT * i

                def pair(c, r, more, it):
                    for s in range(2):
                        if s == 0:
                            landed(pe, "a", n0 + 2 * r, more)
                            landed(pe, "a", n0 + 2 * r + 1, more)
                        if it is not None or r > 0:
                            pe.wait_ge(g, c * 2 + (base + s - 1))
                        for which, sm in enumerate((a, b)):
                            w = chunk("a", n0 + 2 * r + which)
                            for k in range(KT):
                                x = mm(bank[2 * s + which][:], w[:, k, P * s:P * s + P], U[:, k],
                                       start=(k == 0), stop=(k == KT - 1))
                            x.then_inc(sm, 1)

                pe.wait_ge(sem("u"), 8 * (0 if i == 0 else 2) + 8)
                pair(0, 0, 0, None)
                with pe.Fori(0, 3) as it:
                    for r in range(3):
                        pair(it * 3 + (1 + r), 1 + r, it * 16, it)
                pair(10, 10, 0, None)
                pe.wait_ge(g, base + FT)
                outproj(f"ffn{i}_out", FT, "a", lambda k: G[:, k])

            def outproj(name, kts, which, rhs):
                n = first[name]
                for half in range(2):
                    for k0 in range(0, kts, 4):
                        landed(pe, which, n)
                        w = chunk(which, n)
                        for k in range(k0, min(k0 + 4, kts)):
                            for d in range(4):
                                x = mm(bank[4 * half + d][:], w[:, k - k0, P * d:P * d + P], rhs(k),
                                       start=(k == 0), stop=(k == kts - 1))
                        x.then_inc(sem(name + "_used"), 1)
                        n += 1

            norm(0, 0)
            ffn(0)
            norm(1, 0)
            pe.wait_ge(sem("u"), 16)
            n0 = first["mix"]

            def rot(r):
                pe.wait_ge(sem("mix_evac"), r + 3)
                if r >= 2:
                    pe.wait_ge(sem("rope"), r - 1)
                src = Q[:, r] if r < 6 else K[:, r - 6]
                mm(bank[4 + r % 2][:], rotm, src, start=True, stop=True).then_inc(sem("rot"), 1)

            pe.wait_ge(sem("mix_const"), 80)
            m = 0
            for c in range(18):
                landed(pe, "a", n0 + c)
                w = chunk("a", n0 + c)
                if 7 <= c < 10:
                    for t in range(TT):
                        pe.wait_ge(sem("mix_evac"), m - 3)
                        for k in range(KT):
                            lhs = U[:, k, P * t:P * t + P] if c == 7 else U[:, k, t:SEQ:CLASSES]
                            x = mm(bank[m % 4][:, 0:256], lhs, w[:, k, :], start=(k == 0), stop=(k == KT - 1))
                        x.then_inc(sem("mix_tile"), 1)
                        m += 1
                        r = m - 5
                        if 0 <= r < 12:
                            rot(r)
                    continue
                for j in range(2):
                    if m >= 4:
                        pe.wait_ge(sem("mix_evac"), m - 3)
                    for k in range(KT):
                        x = mm(bank[m % 4][:], w[:, k, P * j:P * j + P], U[:, k], start=(k == 0), stop=(k == KT - 1))
                    x.then_inc(sem("mix_tile"), 1)
                    m += 1
                    r = m - 5
                    if 0 <= r < 12:
                        rot(r)
            pe.wait_ge(sem("pool_d"), 1)
            pe.wait_ge(sem("wpool"), 64)
            for k in range(2):
                mm(bank[6 + k][:], wpool[:, k], PD[:, k], start=True, stop=True).then_inc(sem("yp_mm"), 1)

            def scores(u):
                h, c = u // CLASSES, u % CLASSES
                r = 64 * (h % 2)
                R = slice(r, r + 64)
                lo, hi = bank[2 * (u % 2)], bank[2 * (u % 2) + 1]
                if u >= 2:
                    pe.wait_ge(sem("att_s"), u - 1)
                q = lambda g: Q[R, 2 * g + h // 2, c:SEQ:CLASSES]
                k = lambda g: K[R, 2 * g + h // 2, c:SEQ:CLASSES]
                mm(lo[:], q(0), K[R, h // 2, :], start=True, stop=True)
                mm(hi[:, 0:P], q(1), k(1), start=True, stop=True)
                mm(hi[:, P:2 * P], q(2), k(2), start=True, stop=True).then_inc(sem("att_mm"), 1)

            def values(u):
                h, c = u // CLASSES, u % CLASSES
                r = 64 * (h % 2)
                pe.wait_ge(sem("att_pt"), u + 1)
                if u >= 2:
                    pe.wait_ge(sem("att_y"), u - 1)
                for j in range(6):
                    v = V[:, 0, j] if j < 4 else V[:, j - 3, c]
                    x = mm(bank[6 + u % 2][r:r + 64, 0:P], v[:, 64 * h:64 * h + 64], PT1[:, j],
                           start=(j == 0), stop=(j == 5))
                x.then_inc(sem("att_pv"), 1)

            pe.wait_ge(sem("mix_evac"), 42)
            pe.wait_ge(sem("rope"), 12)
            pe.wait_ge(sem("yp"), 2)
            scores(0)
            for u in range(16):
                if u + 1 < 16:
                    scores(u + 1)
                pe.wait_ge(sem("att_p"), u + 1)
                if u:
                    pe.wait_ge(sem("att_pt"), u)
                for j in range(6):
                    dst = bank[4][:, P * j:P * j + P] if j < 4 else bank[5][:, P * (j - 4):P * (j - 3)]
                    x = tp(dst, S1[:, u % 2, P * j:P * j + P], ident)
                x.then_inc(sem("att_tp"), 1)
                values(u)
            n = first["branch"]
            landed(pe, "a", n)
            landed(pe, "a", n + 1)
            pe.wait_ge(sem("att_y"), 16)
            pe.wait_ge(sem("att_s"), 16)
            for d in range(KT):
                if d >= 2:
                    pe.wait_ge(sem("merged"), d - 1)
                for b, y in enumerate((YP, YA)):
                    for k in range(2):
                        x = mm(bank[(2 * d + b) % 4][:], chunk("a", n + b)[:, k, P * d:P * d + P], y[:, k],
                               start=(k == 0), stop=(k == 1))
                x.then_inc(sem("merge_ab"), 1)
            pe.wait_ge(sem("merged"), 8)
            outproj("mix_out", KT, "a", lambda k: MG[:, k])
            norm(2, 0)
            ffn(1)
            norm(3, 0)
            pe.wait_ge(sem("u"), 32)
            n0 = first["conv"]
            for j in range(4):
                for s in range(2):
                    d = 2 * j + s
                    if d >= 2:
                        pe.wait_ge(sem("conv_bc"), d - 1)
                    for which in range(3):
                        landed(pe, "a", n0 + 3 * j + which)
                        w = chunk("a", n0 + 3 * j + which)
                        for k in range(KT):
                            x = mm(bank[3 * s + which][:], w[:, k, P * s:P * s + P], U[:, k],
                                   start=(k == 0), stop=(k == KT - 1))
                        x.then_inc(sem(("conv_c", "conv_h", "conv_b")[which]), 1)
            pe.wait_ge(sem("conv_bc"), 8)
            outproj("conv_out", KT, "a", lambda k: BC[:, k])
            norm(4, 1)

            def to_tokens(n, ready):
                pe.wait_ge(sem("u"), ready)
                for g in range(8):
                    if g >= 4:
                        pe.wait_ge(sem("xt"), 8 * n + g - 3)
                    t, half = g // 2, g % 2
                    for k in range(4):
                        x = tp(bank[g % 4][:, P * k:P * k + P], U[:, 4 * half + k, P * t:P * t + P], ident)
                    x.then_inc(sem("xt_tp"), 1)

            def moe(l):
                to_tokens(l, 40 + 16 * l)
                pe.wait_ge(sem("rows"), 16 * 11)
                for t in range(TT):
                    for k in range(KT):
                        x = mm(bank[4][:, 72 * t:72 * t + 72], U[:, k, P * t:P * t + P], rw[:, l, k],
                               start=(k == 0), stop=(k == KT - 1))
                x.then_inc(sem("moe_logits"), 1)
                EA = RK[:, 1024:1280]
                pe.wait_ge(sem("moe_ea"), l + 1)
                for t in range(TT):
                    for j in range(t + 1):
                        mm(bank[5][:, 64 * t:64 * t + 64], before if j == t else ones[:], EA[:, 64 * j:64 * j + 64],
                           start=(j == 0), stop=(j == t))
                for j in range(TT):
                    x = mm(bank[5][:, 256:320], ones[:], EA[:, 64 * j:64 * j + 64], start=(j == 0), stop=(j == 3))
                x.then_inc(sem("moe_rank"), 1)
                pe.wait_ge(sem("moe_sel"), 4 * l + 4)
                pe.wait_ge(sem("xt"), 8 * l + 8)
                for g in range(16):
                    c, k = g // 8, g % 8
                    if g >= 4:
                        pe.wait_ge(sem("moe_xst"), 16 * l + g - 3)
                    for t in range(TT):
                        x = mm(bank[g % 4][:], XT[:, t, P * k:P * k + P], SEL[:, t, 512 * c:512 * c + 512],
                               start=(t == 0), stop=(t == TT - 1))
                    x.then_inc(sem("moe_gather"), 1)
                pe.wait_ge(sem("moe_xst"), 16 * l + 16)
                pe.wait_ge(sem("moe_plan"), l + 1)
                n = pe.value_load(plan[0:1, 1:2], min_val=EXPERTS // 2, max_val=MAX_ROUNDS * EXPERTS // 2)
                with pe.Fori(0, n) as i:
                    for s in range(2):
                        e = i * 2 + s
                        pe.wait_ge(sem(f"moe{l}_xw"), e + 1)
                        for which in range(2):
                            pe.wait_ge(sem(f"w_m{l}{3 * s + which}"), i * 16 + 16)
                            w = wview(3 * s + which, KT, D_EXP)
                            for f in range(2):
                                for k in range(KT):
                                    x = mm(bank[2 * which + s][:, WIN * f:WIN * f + WIN], w[:, k, P * f:P * f + P],
                                           XW[:, s, k], start=(k == 0), stop=(k == KT - 1))
                            x.then_inc(sem(f"moe{l}_{'ab'[which]}"), 1)
                        pe.wait_ge(sem(f"moe{l}_h"), e + 1)
                        pe.wait_ge(sem(f"moe{l}_add"), e)
                        pe.wait_ge(sem(f"w_m{l}{3 * s + 2}"), i * 16 + 16)
                        w = wview(3 * s + 2, 2, D)
                        for d in range(KT):
                            for f in range(2):
                                x = mm(bank[4 + s][:, WIN * d:WIN * d + WIN], w[:, f, P * d:P * d + P],
                                       HM[:, s, WIN * f:WIN * f + WIN], start=(f == 0), stop=(f == 1))
                        x.then_inc(sem(f"moe{l}_y"), 1)
                pe.wait_ge(sem(f"moe{l}_add"), n * 2 + 1)
                for g in range(8):
                    if g >= 4:
                        pe.wait_ge(sem("moe_swt"), 8 * l + g - 3)
                    for t in range(TT):
                        x = tp(bank[4 + g % 4][:, P * t:P * t + P], SELW[:, t, P * g:P * g + P], ident)
                    x.then_inc(sem("moe_swtp"), 1)
                for g in range(16):
                    st_, half = g // 2, g % 2
                    if g >= 4:
                        pe.wait_ge(sem("moe_ys"), 16 * l + g - 3)
                    for k in range(4):
                        x = tp(bank[g % 4][:, P * k:P * k + P], YST[:, 4 * half + k, P * st_:P * st_ + P], ident)
                    x.then_inc(sem("moe_ystp"), 1)
                pe.wait_ge(sem("moe_swt"), 8 * l + 8)
                pe.wait_ge(sem("moe_ys"), 16 * l + 16)
                for d in range(KT):
                    if d >= 4:
                        pe.wait_ge(sem("h"), 32 + 16 * l + d - 3)
                    for s in range(8):
                        x = mm(bank[d % 4][:], YS[:, s, P * d:P * d + P], SWT[:, s], start=(s == 0), stop=(s == 7))
                    x.then_inc(sem("moe_f"), 1)

            moe(0)
            norm(5, 2)
            pe.wait_ge(sem("bkt"), 32)
            pe.wait_ge(sem("u"), 48)
            mm(bank[6][0:HEADS2, :], RB[0:BUCKETS], BKT[0:BUCKETS, 0:512], start=True, stop=True)
            mm(bank[7][0:HEADS2, 0:P], RB[0:BUCKETS], BKT[0:BUCKETS, 512:640], start=True, stop=True)\
                .then_inc(sem("vb_mm"), 1)
            def qi(b, w, c0):
                for k in range(KT):
                    x = mm(bank[b][:], w[:, k, c0:c0 + P], U[:, k], start=(k == 0), stop=(k == KT - 1))
                return x

            landed(pe, "b", 0)
            w = chunk("b", 0)
            for t in range(TT):
                for k in range(KT):
                    x = mm(bank[4][:, P * t:P * t + P], U[:, k, P * t:P * t + P], w[:, k, 0:P],
                           start=(k == 0), stop=(k == KT - 1))
            x.then_inc(sem("kv_mm"), 1)
            qi(0, w, P).then_inc(sem("qi_mm"), 1)
            landed(pe, "b", 1)
            qi(1, chunk("b", 1), 0).then_inc(sem("qi_mm"), 1)
            qi(2, chunk("b", 1), P).then_inc(sem("qi_mm"), 1)
            landed(pe, "b", 2)
            w = chunk("b", 2)
            qi(3, w, 0).then_inc(sem("qi_mm"), 1)
            for t in range(TT):
                for k in range(KT):
                    x = mm(bank[5][:, 72 * t:72 * t + 72], U[:, k, P * t:P * t + P], w[:, k, P:200],
                           start=(k == 0), stop=(k == KT - 1))
            x.then_inc(sem("ki_mm"), 1)
            pe.wait_ge(sem("ckv"), 4)
            pe.wait_ge(sem("vb"), 2)
            for t in range(TT):
                x = tp(bank[6][:, P * t:P * t + P], CKV[:, t], ident)
            x.then_inc(sem("kv_tp"), 1)
            pe.wait_ge(sem("ki"), 4)
            for t in range(TT):
                x = tp(bank[7][:, P * t:P * t + P], KI[:, t], ident)
            x.then_inc(sem("kv_tp"), 1)
            pe.wait_ge(sem("kvt"), 2)
            pe.wait_ge(sem("qi"), 4)
            m = 0
            for qb in range(1, TT):
                for h in range(IDX_HEADS):
                    if m >= 4:
                        pe.wait_ge(sem("idx_relu"), m - 3)
                    R = slice(64 * (h % 2), 64 * (h % 2) + 64)
                    n = (qb + 1) * P
                    mm(bank[m % 4][:, 0:n], QI[R, h // 2, P * qb:P * qb + P], KIT[R, 0:n], start=True, stop=True)\
                        .then_inc(sem("idx_mm"), 1)
                    m += 1
            for c in range(8):
                landed(pe, "b", 3 + c)
                for j in range(2):
                    h = 2 * c + j
                    if h >= 4:
                        pe.wait_ge(sem("q2"), h - 3)
                    qi(4 + h % 4, chunk("b", 3 + c), P * j).then_inc(sem("dsa_q"), 1)
            units = [(qb, h) for qb in range(TT) for h in range(HEADS2)]

            def logits(u):
                qb, h = units[u]
                n = (qb + 1) * P
                if u >= 2:
                    pe.wait_ge(sem("ds_s"), u - 1)
                mm(bank[u % 2][:, 0:n], Q2[:, h, qb * P:qb * P + P], CKVT[:, 0:n], start=True, stop=True)\
                    .then_inc(sem("ds_mm"), 1)

            pe.wait_ge(sem("q2"), 16)
            pe.wait_ge(sem("idx_relu"), 24)
            logits(0)
            for u, (qb, h) in enumerate(units):
                if u + 1 < len(units):
                    logits(u + 1)
                pe.wait_ge(sem("ds_p"), u + 1)
                if u >= 2:
                    pe.wait_ge(sem("ds_pt"), u - 1)
                for j in range(qb + 1):
                    x = tp(bank[2 + u % 2][:, P * j:P * j + P], S2[:, u % 2, P * j:P * j + P], ident)
                x.then_inc(sem("ds_tp"), 1)
                pe.wait_ge(sem("ds_pt"), u + 1)
                if u >= 2:
                    pe.wait_ge(sem("ds_o"), u - 1)
                for j in range(qb + 1):
                    x = mm(bank[4 + u % 2][:, 0:P], CKV[:, j], PT2[:, u % 2, P * j:P * j + P],
                           start=(j == 0), stop=(j == qb))
                x.then_inc(sem("ds_pv"), 1)
            pe.wait_ge(sem("ds_o"), 64)
            outproj("dsa_out", HEADS2, "b", lambda k: Q2[:, k])
            norm(6, 3)
            moe(1)
            norm(7, 4)
            to_tokens(2, 64)


_WEIGHTS = ["x", "positions", "w_ada", "w_ffn1_in", "w_ffn1_out", "w_in", "w_pool", "w_pool_branch",
            "w_attn_branch", "w_out", "w_ffn2_in", "w_ffn2_out"]
_WEIGHTS2 = ["conv_w_in", "conv_w_out", "attn_w_in", "kv_norm_g", "kidx_ln_g", "kidx_ln_b", "attn_w_out",
             "rel_bias", "router_wg", "router_bg", "router_we", "router_be", "exp_w1", "exp_w3", "exp_w2"]
_SQUEEZE = {"w_ada", "w_ffn1_in", "w_ffn1_out", "w_in", "w_pool", "w_pool_branch", "w_attn_branch", "w_out",
            "w_ffn2_in", "w_ffn2_out", "conv_w_in", "conv_w_out", "attn_w_in", "attn_w_out"}


def kernel(**inputs):
    import numpy as _np
    import concourse.bacc as _bacc
    from concourse import mybir as _mybir
    from concourse.bass_utils import run_bass_kernel_spmd as _run

    nc = _bacc.Bacc("TRN2", target_bir_lowering=False, num_devices=1)
    arrays, A = {}, {}

    def give(name, a):
        a = _np.ascontiguousarray(a)
        arrays[f"in_{name}"] = a
        A[name] = nc.dram_tensor(f"in_{name}", a.shape, _mybir.dt.from_np(a.dtype), kind="ExternalInput").ap()

    for name in _WEIGHTS + _WEIGHTS2:
        a = _np.asarray(inputs[name if name in _WEIGHTS else name + "_2"])
        give(name, a[0] if name in _SQUEEZE else a)
    parts = []
    for name in ("b_ada", "g_norm_ffn1", "g_norm_mix", "g_norm_ffn2", "g_final", "c", "pool_scale",
                 "conv_k_2", "ln1_g_2", "ln1_b_2", "ln2_g_2", "ln2_b_2"):
        parts.append(_np.asarray(inputs[name]).reshape(-1, P).T)
    give("params", _np.concatenate(parts, axis=1))
    give("consts", constants())
    out = nc.dram_tensor("out_0_dram", (1, SEQ, D), F32, kind="ExternalOutput").ap()
    build(nc, A, out)
    r = _run(nc, [arrays], core_ids=[0])
    return r.results[0]["out_0_dram"]
```

```python
from contextlib import ExitStack

import numpy as np

import concourse.bass as bass
from concourse import mybir

F32 = mybir.dt.float32
I32 = mybir.dt.int32
U32 = mybir.dt.uint32
F32R = mybir.dt.float32r
ALU = mybir.AluOpType
ACT = mybir.ActivationFunctionType
AXX = mybir.AxisListType.X

P = 128
SEQ = 512
D = 1024
KT = D // P
TT = SEQ // P
FF = 2816
FT = FF // P
HEAD = 64
POOL_W = 256
ATT_W = 768
N_MOD = 9
CLASSES = 4
RMS_EPS = 1e-6
LN_EPS = 1e-5
ALPHA = (2.0 * 2) ** 0.25
NEG = -1e30
TAKEN = -3e38
IDX_HEADS = 8
IDX_DIM = 64
LATENT = 128
HEADS2 = 16
TOPK = SEQ // 4
BUCKETS = 32
EXPERTS = 64
GROUPS = 8
PER_GROUP = 8
D_EXP = 256
PAIRS = 2 * SEQ
WIN = 64
SLOTS = PAIRS + WIN
MAX_ROUNDS = SEQ // WIN
RING = 6
CHUNK = 2048
WBUF = 3
ADA_FIRST = 12
ADA_ALL = 36

PC = {}
_at = 0
for _name, _n in (("b_ada", 72), ("g_ffn1", 8), ("g_mix", 8), ("g_ffn2", 8), ("g_final", 8), ("c", 8),
                  ("pool_scale", 2), ("conv_k", 24), ("ln1_g", 16), ("ln1_b", 16), ("ln2_g", 16), ("ln2_b", 16)):
    PC[_name] = _at
    _at += _n
N_PARAM = _at

CC = {}
_at = 0
for _name, _n in (("ident", P), ("causal", P), ("before", P), ("slot", PAIRS), ("lane", 2 * WIN), ("invf", 1), ("lanecol", 1),
                  ("rot", P), ("mod4", P), ("band", CLASSES * SEQ), ("recip", 2 * SEQ), ("bucket", 640)):
    CC[_name] = _at
    _at += _n
N_CONST = _at
N_KEEP = CC["rot"]


def constants():
    c = np.zeros((P, N_CONST), np.float32)
    p = np.arange(P)[:, None]
    q = np.arange(P)[None, :]

    def put(name, a):
        c[:a.shape[0], CC[name]:CC[name] + a.shape[1]] = a

    put("ident", (p == q).astype(np.float32))
    put("causal", np.where(q <= p, 0.0, NEG))
    put("before", (p < q).astype(np.float32))
    put("slot", np.broadcast_to(np.arange(PAIRS), (P, PAIRS)))
    put("lane", np.broadcast_to(np.arange(2 * WIN) % WIN, (P, 2 * WIN)))
    rot = np.zeros((P, P))
    for m in range(P):
        if m % HEAD < HEAD // 2:
            rot[m + HEAD // 2, m] = -1.0
        else:
            rot[m - HEAD // 2, m] = 1.0
    put("rot", rot)
    put("mod4", np.where((q <= p) & ((p - q) % 4 == 0), 0.0, NEG))
    s = np.arange(SEQ)[None, :]
    for k in range(CLASSES):
        d = k + CLASSES * p - s
        c[:, CC["band"] + k * SEQ:CC["band"] + (k + 1) * SEQ] = np.where((d >= 0) & (d <= 128), 0.0, NEG)
    t = np.arange(SEQ)
    for tile in range(2):
        for half in range(2):
            w = 2 ** (1 + 2 * tile + half)
            at = CC["recip"] + tile * SEQ
            c[64 * half:64 * half + 64, at:at + SEQ] = (np.float32(1) / np.minimum(t + 1, w).astype(np.float32))[None]
    inv = np.float32(10000.0) ** (-np.arange(0, HEAD, 2, dtype=np.float32) / np.float32(HEAD))
    c[:, CC["invf"]] = np.tile(inv, P // 32)
    put("lanecol", p % WIN)
    dist = np.maximum(SEQ - 1 - np.arange(640), 0)
    large = 16 + (np.log(np.maximum(dist, 1).astype(np.float32) / np.float32(16)) / np.float32(np.log(8.0))
                  * np.float32(16)).astype(np.int32)
    bucket = np.where(dist < 16, dist, np.minimum(large, BUCKETS - 1))
    put("bucket", (np.arange(BUCKETS)[:, None] == bucket[None, :]).astype(np.float32))
    return c


class Steps:

    def __init__(self, eng, sem):
        self.eng, self.sem, self.n = eng, sem, 0

    def did(self, ins):
        self.n += 1
        ins.then_inc(self.sem, 1)

    def wait(self):
        self.eng.wait_ge(self.sem, self.n)


def build(nc, A, out):
    with ExitStack() as ctx:
        def sb(name, shape, dt=F32):
            return ctx.enter_context(nc.sbuf_tensor(name, shape, dt))

        _sems = {}

        def sem(name):
            if name not in _sems:
                _sems[name] = ctx.enter_context(nc.semaphore(name))
            return _sems[name]

        H = sb("H", [P, KT, SEQ])
        U = sb("U", [P, KT, SEQ])
        keep = sb("keep", [P, N_KEEP])
        par = sb("par", [P, N_PARAM])
        mod = sb("mod", [P, 72])
        gains = sb("gains", [P, 24])
        gates = sb("gates", [P, 24])
        csil = sb("csil", [P, KT])
        kvg = sb("kvg", [P, LATENT])
        lng = sb("lng", [P, IDX_DIM])
        lnb = sb("lnb", [P, IDX_DIM])
        rbias = sb("rbias", [P, 2, 72])
        rw = sb("rw", [P, 2, KT, 72])
        ones = sb("ones", [P, P])
        epsc = sb("epsc", [P, 3])
        rstd = sb("rstd", [P, SEQ])
        small = sb("small", [P, 64])
        with nc.sbuf_tensor("arena", [P, 28544], F32) as arena, nc.sbuf_tensor("ring", [P, RING, CHUNK], F32) as ring:
            pass
        parts = sb("parts", [P, 28544], F32R)
        ring_low = sb("ring_low", [P, RING, CHUNK], F32R)
        bank = [ctx.enter_context(nc.psum_tensor(f"bank{i}", [P, 512], F32)) for i in range(8)]

        ident = keep[:, CC["ident"]:CC["ident"] + P]
        causal = keep[:, CC["causal"]:CC["causal"] + P]
        before = keep[:, CC["before"]:CC["before"] + P]
        slotrow = keep[:, CC["slot"]:CC["slot"] + PAIRS]
        invf = keep[:, CC["invf"]:CC["invf"] + 1]
        lanecol = keep[:, CC["lanecol"]:CC["lanecol"] + 1]
        lane = keep[:, CC["lane"]:CC["lane"] + 2 * WIN]

        def area(at, *shape):
            n = int(np.prod(shape))
            assert at + n <= 28544, (at, shape)
            v = arena[:, at:at + n]
            if len(shape) == 2:
                v = v.rearrange("p (a b) -> p a b", a=shape[0])
            if len(shape) == 3:
                v = v.rearrange("p (a b c) -> p a b c", a=shape[0], b=shape[1])
            return v

        def rounded(at, a, b):
            assert at + a * b <= 28544
            return parts[:, at:at + a * b].rearrange("p (a b) -> p a b", a=a)

        def col(name, i=0):
            return par[:, PC[name] + i:PC[name] + i + 1]

        spread = nc.dram_tensor("bias_spread", [P, HEADS2, 640], F32, kind="Internal").ap()
        scratch = nc.dram_tensor("bias_rows", [HEADS2, 640], F32, kind="Internal").ap()

        xtok = area(0, TT, D)
        G = area(0, FT, SEQ)
        AC = area(11264, 2, 2, 256)
        UP = (rounded(12288, KT, SEQ), rounded(16384, KT, SEQ))
        UP_MIX = (rounded(4096, KT, SEQ), rounded(9728, KT, SEQ))
        WHI = rounded(20480, WBUF, CHUNK)
        Q = area(0, 6, SEQ)
        K = area(3072, 6, SEQ)
        MG = area(0, KT, SEQ)
        V = area(6144, 3, TT, 256)
        S1 = area(9216, 3, 768)
        PT1 = area(11520, 2, 768)
        PB = area(9216, 2, 528)
        PS2 = area(10272, 2, 528)
        PS4 = area(11328, 2, 528)
        PRC = area(12384, 2, SEQ)
        PD = area(13408, 2, SEQ)
        GT = area(14432, 16, SEQ)
        cosT = area(22624, SEQ)
        sinT = area(23136, SEQ)
        band = area(23648, CLASSES, SEQ)
        mod4 = area(25696, P)
        rotm = area(25824, P)
        wpool = area(25952, 2, P)
        YA = area(26208, 2, SEQ)
        YP = area(27232, 2, SEQ)
        RT = area(26208, 2, SEQ)
        RT2 = area(9216, SEQ)
        posi = arena[:, 0:SEQ].bitcast(I32)
        TB = area(512, 6, SEQ)
        CG = area(0, 2, SEQ)
        CU = area(1024, 2, SEQ + 2)
        CV = area(2056, 2, SEQ)
        BC = area(3080, KT, SEQ)
        XT = area(0, TT, D)
        SEL = area(4096, TT, PAIRS)
        YST = area(0, KT, SLOTS)
        XST = area(8704, KT, SLOTS)
        SELW = area(17408, TT, PAIRS)
        XW = area(21504, 2, KT, WIN)
        SA = area(22528, 2, 2 * WIN)
        HB = area(22784, 2, 2 * WIN)
        HM = area(23040, 2, 2 * WIN)
        YS = area(8704, 8, D)
        SWT = area(23296, 8, SEQ)
        LG = area(23296, TT, 72)
        RK = area(23600, 2048)
        SELT = area(25648, PAIRS)
        REM = area(27392, MAX_ROUNDS * EXPERTS)
        startf = area(27904, EXPERTS)
        STI = arena[:, 27968:27968 + MAX_ROUNDS * EXPERTS].bitcast(I32)
        plan = arena[:, 28480:28485].bitcast(I32)
        Q2 = area(0, HEADS2, SEQ)
        TOE = area(8192, HEADS2, SEQ)
        CKV = area(16384, TT, LATENT)
        CKVT = area(16896, SEQ)
        SM = area(17408, 3, SEQ)
        QI = area(18944, 4, SEQ)
        KI = area(20992, TT, P)
        KIT = area(21504, SEQ)
        IR = area(22016, 2, SEQ)
        S2 = area(23040, 3, SEQ)
        PT2 = area(24576, 2, SEQ)
        VB = area(25600, 640)
        BKT = area(26240, 640)
        RB = area(26880, 16)
        W8 = area(26896, TT, 8)
        DS = area(26928, 512)

        def tall(w, c0, n):
            return w[:, c0:c0 + n].rearrange("(k p) n -> p k n", p=P)

        def flat(w, k0, nk, c0, n):
            return w[k0 * P:(k0 + nk) * P, c0:c0 + n].rearrange("(k p) n -> p k n", p=P)

        stream_a, stream_b = [], []

        def ffn_at(i, c):
            return first[f"ffn{i}"] + (2 * c if i else (0 if c == 0 else 5 + 4 * (c - 1)))

        def ada_of(c):
            a = ADA_FIRST + (0 if c == 0 else 3 + 2 * (c - 1))
            return list(range(a, a + (3 if c in (0, 10) else 2)))

        first = {}

        def outs(stream, name, w, kts):
            first[name] = len(stream)
            n = 0
            for half in range(2):
                for k0 in range(0, kts, 4):
                    n += 1
                    nk = min(4, kts - k0)
                    stream.append((flat(w, k0, nk, 512 * half, 512), nk, 512, name + "_used", n))

        first["ada"] = 0

        def ada_chunks(n):
            for _ in range(n):
                a = first["ada"]
                stream_a.append((tall(A["w_ada"], 256 * a, 256), KT, 256, "ada_step", 8 * a + 8))
                first["ada"] += 1

        ada_chunks(ADA_FIRST)
        def ffn_stream(i):
            first[f"ffn{i}"] = len(stream_a)
            w = A[f"w_ffn{i + 1}_in"]
            for c in range(FT // 2):
                stream_a.append((tall(w, 256 * c, 256), KT, 256, "ffn_a", FT * i + 2 * c + 2))
                stream_a.append((tall(w, FF + 256 * c, 256), KT, 256, "ffn_b", FT * i + 2 * c + 2))
                if i == 0:
                    ada_chunks(3 if c in (0, 10) else 2)
            outs(stream_a, f"ffn{i}_out", A[f"w_ffn{i + 1}_out"], FT)

        ffn_stream(0)
        first["mix"] = len(stream_a)
        mix_tiles = [2, 4, 6, 8, 10, 12, 14, 18, 22, 26] + [28 + 2 * i for i in range(8)]
        for c, n in enumerate(mix_tiles):
            stream_a.append((tall(A["w_in"], 256 * c, 256), KT, 256, "mix_tile", n))
        first["branch"] = len(stream_a)
        stream_a.append((flat(A["w_pool_branch"], 0, 2, 0, 1024), 2, 1024, "merge_ab", 8))
        stream_a.append((flat(A["w_attn_branch"], 0, 2, 0, 1024), 2, 1024, "merge_ab", 8))
        outs(stream_a, "mix_out", A["w_out"], KT)
        ffn_stream(1)
        first["conv"] = len(stream_a)
        for j in range(4):
            for which, at in enumerate((1024, 2048, 0)):
                stream_a.append((tall(A["conv_w_in"], at + 256 * j, 256), KT, 256,
                                 ("conv_c", "conv_h", "conv_b")[which], 2 * j + 2))
        outs(stream_a, "conv_out", A["conv_w_out"], KT)
        first["dsa"] = 0
        for n, c in enumerate((8, 9, 10)):
            stream_b.append((tall(A["attn_w_in"], 256 * c, 256 if c < 10 else 200), KT, 256 if c < 10 else 200,
                             ("qi_mm", "qi_mm", "ki_mm")[n], (1, 3, 1)[n]))
        for c in range(8):
            stream_b.append((tall(A["attn_w_in"], 256 * c, 256), KT, 256, "dsa_q", 2 * c + 2))
        outs(stream_b, "dsa_out", A["attn_w_out"], HEADS2)
        streams = {"a": stream_a, "b": stream_b}
        assert len(stream_a) % RING == 0

        splits, split_at = [], {}
        for name, which, ns in [
                ("ffn0", "a", [ffn_at(0, c) + w for c in range(FT // 2) for w in range(2)]),
                ("ffn0_out", "a", range(first["ffn0_out"], first["ffn0_out"] + 12)),
                ("mix_out", "a", range(first["mix_out"], first["mix_out"] + 4)),
                ("ffn1", "a", [ffn_at(1, c) + w for c in range(FT // 2) for w in range(2)]),
                ("ffn1_out", "a", range(first["ffn1_out"], first["ffn1_out"] + 12)),
                ("conv", "a", range(first["conv"], first["conv"] + 12)),
                ("conv_out", "a", range(first["conv_out"], first["conv_out"] + 4)),
                ("dsa_out", "b", range(first["dsa_out"], first["dsa_out"] + 8))]:
            split_at[name] = len(splits)
            splits += [(which, n) for n in ns]
        tiles_at, n_ = {}, 0
        for name, m in (("ffn0", KT), ("ffn0_out", 2 * FT), ("mix_out", KT), ("ffn1", KT), ("ffn1_out", 2 * FT),
                        ("conv", KT), ("conv_out", KT), ("dsa_out", 2 * HEADS2)):
            tiles_at[name] = n_
            n_ += m

        def high(i):
            which, n = splits[i]
            _, nk, cols, _, _ = streams[which][n]
            buf = WHI[:, i % WBUF, 0:nk * cols]
            return buf, nk, cols

        def both(i):
            buf, nk, cols = high(i)
            low = ring_low[:, splits[i][1] % RING, 0:nk * cols]
            return [v.rearrange("p (k n) -> p k n", k=nk) for v in (buf, low)]

        def wview(slot, nk, n):
            return ring[:, slot, 0:nk * n].rearrange("p (k n) -> p k n", k=nk)

        def chunk(which, n):
            _, nk, cols, _, _ = streams[which][n]
            return wview(n % RING, nk, cols)

        def landed(eng, which, n, more=0):
            n += len(stream_a) if which == "b" else 0
            eng.wait_ge(sem(f"w_{n % RING}"), 16 * (n // RING + 1) + more)

        block = ctx.enter_context(nc.Block())

        def ends(eng):
            return [eng.value_load(plan[0:1, c:c + 1], min_val=EXPERTS - 2, max_val=MAX_ROUNDS * EXPERTS - 1)
                    for c in (4, 2)]

        @block.sync
        def _(sp):
            def load(which, n):
                src, nk, cols, _, _ = streams[which][n]
                sp.dma_start(wview(n % RING, nk, cols), src).then_inc(sem(f"w_{n % RING}"), 16)

            def matrix(layer, j, e, q, s):
                w = ("exp_w1", "exp_w3", "exp_w2")[j]
                one = A[w][layer, e:e + 1] if isinstance(e, int) else A[w][layer, bass.ds(e, 1)]
                slot = 3 * (s % 2) + j
                nk, cols = (KT, D_EXP) if j < 2 else (2, D)
                sp.wait_ge(sem(f"moe{layer}_{('ab', 'ab', 'y')[j]}"), q * 2 + (s - 1))
                sp.dma_start(wview(slot, nk, cols), one.rearrange("a (k p) n -> p (a k) n", p=P))\
                  .then_inc(sem(f"w_m{layer}{slot}"), 16)

            def experts(layer, e, q):
                for s in (1, 2):
                    matrix(layer, 0, e + s, q, s)
                    matrix(layer, 1, e + s, q, s)
                    matrix(layer, 2, e + (s - 1), q, s - 1)

            for n in range(len(stream_a)):
                if n >= RING:
                    _, _, _, s, v = stream_a[n - RING]
                    sp.wait_ge(sem(s), v)
                load("a", n)

            rounds = None
            for layer in range(2):
                prev = streams["ab"[layer]]
                used = {}
                for n in range(len(prev)):
                    used[n % RING] = prev[n][3:]
                for slot in (0, 1, 3, 4, 2, 5):
                    s, v = used[slot]
                    sp.wait_ge(sem(s), v)
                    j = slot % 3
                    w = ("exp_w1", "exp_w3", "exp_w2")[j]
                    nk, cols = (KT, D_EXP) if j < 2 else (2, D)
                    sp.dma_start(wview(slot, nk, cols), A[w][layer, slot // 3].rearrange("(k p) n -> p k n", p=P))\
                      .then_inc(sem(f"w_m{layer}{slot}"), 16)
                sp.wait_ge(sem("moe_plan"), layer + 1)
                rounds = sp.value_load(plan[0:1, 0:1], min_val=1, max_val=MAX_ROUNDS)
                half = EXPERTS // 2
                for j in range(2):
                    matrix(layer, j, 2, 1, 0)
                with sp.Fori(0, rounds) as j:
                    with sp.Fori(1, half - 1) as i:
                        experts(layer, i * 2, j * half + i)
                    for m, s in ((0, 1), (1, 1), (2, 0), (2, 1)):
                        matrix(layer, m, EXPERTS - 2 + s, j * half + (half - 1), s)
                    with sp.If(j + 1 < rounds):
                        for m in range(2):
                            matrix(layer, m, 0, j * half + half, 0)
                        experts(layer, 0, j * half + half)
                if layer == 0:
                    last = sp.value_load(plan[0:1, 2:3], min_val=EXPERTS - 1, max_val=MAX_ROUNDS * EXPERTS - 1)
                    every = sp.value_load(plan[0:1, 3:4], min_val=EXPERTS, max_val=MAX_ROUNDS * EXPERTS)
                    for n in range(len(stream_b)):
                        if n < RING:
                            sp.wait_ge(sem(f"moe0_{('ab', 'ab', 'y')[n % 3]}"), last if n < 3 else every)
                        else:
                            _, _, _, s, v = stream_b[n - RING]
                            sp.wait_ge(sem(s), v)
                        load("b", n)
            sp.wait_ge(sem("xt"), 24)
            sp.dma_start(out.rearrange("a (t p) d -> p (a t) d", p=P), XT).then_inc(sem("stored"), 16)
            sp.wait_ge(sem("stored"), 16)

        @block.gpsimd
        def _(pool):
            st = Steps(pool, sem("pool_step"))
            st.did(pool.memset(ones[:], 1.0))
            pool.memset(epsc[:, 0:1], RMS_EPS).then_inc(sem("eps"), 1)
            pool.memset(epsc[:, 1:2], LN_EPS).then_inc(sem("eps"), 1)
            pool.memset(epsc[:, 2:3], 0.0).then_inc(sem("eps"), 1)
            for l in range(2):
                pool.dma_start(rw[:, l, :, 0:GROUPS], A["router_wg"][l].rearrange("(k p) n -> p k n", p=P))\
                    .then_inc(sem("rows"), 16)
                pool.dma_start(rw[:, l, :, GROUPS:72], A["router_we"][l].rearrange("(k p) n -> p k n", p=P))\
                    .then_inc(sem("rows"), 16)
                pool.dma_start(rbias[:, l, 0:GROUPS], A["router_bg"][l].partition_broadcast(P)).then_inc(sem("rows"), 16)
                pool.dma_start(rbias[:, l, GROUPS:72], A["router_be"][l].partition_broadcast(P)).then_inc(sem("rows"), 16)
            pool.dma_start(kvg[:], A["kv_norm_g"][0].partition_broadcast(P)).then_inc(sem("rows"), 16)
            pool.dma_start(lng[:], A["kidx_ln_g"][0].partition_broadcast(P)).then_inc(sem("rows"), 16)
            pool.dma_start(lnb[:], A["kidx_ln_b"][0].partition_broadcast(P)).then_inc(sem("rows"), 16)

            pool.wait_ge(sem("h"), 8)
            mixc = sem("mix_const")
            for name, dst in (("rot", rotm), ("mod4", mod4)):
                pool.dma_start(dst, A["consts"][:, CC[name]:CC[name] + P]).then_inc(mixc, 16)
            pool.dma_start(band, A["consts"][:, CC["band"]:CC["band"] + CLASSES * SEQ]
                           .rearrange("p (a b) -> p a b", a=CLASSES)).then_inc(mixc, 16)
            pool.dma_start(PRC, A["consts"][:, CC["recip"]:CC["recip"] + 2 * SEQ]
                           .rearrange("p (a b) -> p a b", a=2)).then_inc(mixc, 16)
            pool.dma_start(posi, A["positions"][0].partition_broadcast(P)).then_inc(mixc, 16)
            st.did(pool.memset(wpool, 0.0))
            st.wait()
            for g in range(4):
                r = 64 * (g % 2)
                pool.dma_start(wpool[r:r + 64, g // 2, r:r + 64], A["w_pool"][g]).then_inc(sem("wpool"), 16)
            st.did(pool.memset(PB[:, :, 0:16], 0.0))
            st.did(pool.memset(PS2[:, :, 0:16], 0.0))
            st.did(pool.memset(PS4[:, :, 0:16], 0.0))
            pool.wait_ge(sem("mix_evac"), 2)
            pool.wait_ge(mixc, 80)
            st.wait()
            N = slice(16, 528)
            st.did(pool.tensor_tensor(PS2[:, :, N], PB[:, :, N], PB[:, :, 15:527], ALU.add))
            st.wait()
            st.did(pool.tensor_tensor(PS4[:, :, N], PS2[:, :, N], PS2[:, :, 14:526], ALU.add))
            st.wait()
            st.did(pool.tensor_tensor(PD[0:64, 0], PS2[0:64, 0, N], PRC[0:64, 0], ALU.mult))
            st.wait()
            st.did(pool.tensor_tensor(PD[64:P, 0], PS4[64:P, 0, N], PRC[64:P, 0], ALU.mult))
            st.wait()
            st.did(pool.tensor_tensor(PS2[:, 1, N], PS4[:, 1, N], PS4[:, 1, 12:524], ALU.add))
            st.wait()
            st.did(pool.tensor_tensor(PD[0:64, 1], PS2[0:64, 1, N], PRC[0:64, 1], ALU.mult))
            st.wait()
            st.did(pool.tensor_tensor(PS4[64:P, 1, N], PS2[64:P, 1, N], PS2[64:P, 1, 8:520], ALU.add))
            st.wait()
            st.did(pool.tensor_tensor(PD[64:P, 1], PS4[64:P, 1, N], PRC[64:P, 1], ALU.mult))
            st.wait()
            pool.tensor_tensor(PD, PD, PB[:, :, N], ALU.subtract).then_inc(sem("pool_d"), 1)

            for layer in range(2):
                xw, a_b = sem(f"moe{layer}_xw"), sem(f"moe{layer}_ab")
                pool.wait_ge(sem("moe_xst"), 16 * layer + 16)
                pool.wait_ge(sem("moe_tail"), layer + 1)
                pool.wait_ge(sem("moe_plan"), layer + 1)
                n = pool.value_load(plan[0:1, 1:2], min_val=EXPERTS // 2, max_val=MAX_ROUNDS * EXPERTS // 2)

                def window(e, s):
                    at = pool.value_load(STI[0:1, bass.ds(e, 1)] if not isinstance(e, int) else STI[0:1, e:e + 1],
                                         min_val=0, max_val=PAIRS)
                    pool.tensor_copy(XW[:, s], XST[:, :, bass.ds(at, WIN)]).then_inc(xw, 1)

                for s in range(2):
                    window(s, s)
                with pool.Fori(1, n) as i:
                    for s in range(2):
                        pool.wait_ge(a_b, i * 2 + (s - 1))
                        window(i * 2 + s, s)
                if layer == 0:
                    pool.wait_ge(sem("h"), 40)
                    pool.dma_start(BKT[0:BUCKETS], A["consts"][0:BUCKETS, CC["bucket"]:CC["bucket"] + 640])\
                        .then_inc(sem("bkt"), 16)
                    pool.dma_start(RB[0:BUCKETS], A["rel_bias"]).then_inc(sem("bkt"), 16)
                    pool.wait_ge(sem("vb"), 2)
                    pool.dma_start(scratch, VB[0:HEADS2]).then_inc(sem("vb_out"), 16)
                    pool.wait_ge(sem("vb_out"), 16)
                    pool.dma_start(spread, scratch.partition_broadcast(P)).then_inc(sem("spread"), 16)
                    pool.wait_ge(sem("spread"), 16)
                    shifted = bass.AP(spread.tensor, P - 1, [[HEADS2 * 640 - 1, P], [640, HEADS2], [1, SEQ]])
                    pool.dma_start(TOE, shifted).then_inc(sem("toe"), 16)

        @block.scalar
        def _(act):
            st = Steps(act, sem("act_step"))
            A_ = nc.scalar.activation
            act.dma_start(par[:], A["params"]).then_inc(sem("par"), 16)
            act.dma_start(xtok, A["x"].rearrange("a (t p) d -> p (a t) d", p=P)).then_inc(sem("x_in"), 16)
            act.dma_start(keep[:], A["consts"][:, 0:N_KEEP]).then_inc(sem("keep"), 16)

            def evac(dst, src, s):
                A_(dst, src, ACT.Copy).then_inc(sem(s), 1)

            act.wait_ge(sem("par"), 16)
            A_(csil[:], par[:, PC["c"]:PC["c"] + KT], ACT.Silu).then_inc(sem("csil"), 1)
            for k in range(KT):
                act.wait_ge(sem("x_tp"), k + 1)
                evac(H[:, k], bank[k % 4][:], "x_h")

            def weights_high(i, j=None, more=0):
                which, n = splits[i]
                landed(act, which, n, more)
                if i >= WBUF:
                    w, m = splits[i - WBUF]
                    act.wait_ge(sem(streams[w][m][3]), streams[w][m][4] if j is None else j)
                buf, nk, cols = high(i)
                A_(buf, ring[:, n % RING, 0:nk * cols], ACT.Copy).then_inc(sem("w_high"), 1)

            def tile_high(dst, src):
                A_(dst, src, ACT.Copy).then_inc(sem("t_high"), 1)

            def out_high(name, kts, rhs, dst, ready):
                n = 2 * -(-kts // 4)
                for q in range(n):
                    if q or name == "dsa_out" or name == "mix_out":
                        weights_high(split_at[name] + q)
                    if kts > KT or q < n // 2:
                        if kts > KT and q >= 2:
                            act.wait_ge(sem(name + "_used"), q - 1)
                        k0 = 4 * (q % (n // 2))
                        for k in range(k0, min(k0 + 4, kts)):
                            if q < n // 2:
                                ready(k)
                            tile_high(dst[0][:, 4 * (q % 2) + k - k0], rhs(k))

            def norm(i, ln, shift, split=False):
                for k in range(KT):
                    if ln:
                        act.wait_ge(sem("centred"), 8 * (ln - 1) + k + 1)
                    elif k == 0:
                        act.wait_ge(sem("x_h") if i == 0 else sem("h"), 8 if i == 0 else 8 * i)
                    A_(U[:, k], H[:, k], ACT.Square).then_inc(sem("squares"), 1)
                if i == 0:
                    act.wait_ge(sem("eps"), 3)
                act.wait_ge(sem("sumsq"), i + 1)
                if i:
                    act.wait_ge(sem("normed"), 8 * i)
                A_(rstd[:], bank[7][:], ACT.Sqrt, scale=1.0 / D,
                   bias=epsc[:, 1:2] if ln else epsc[:, 0:1]).then_inc(sem("root"), 1)
                for k in range(KT):
                    act.wait_ge(sem("normed"), 8 * i + k + 1)
                    A_(U[:, k], U[:, k], ACT.Identity, bias=shift(k)).then_inc(sem("u"), 1)
                    if split:
                        act.wait_ge(sem("u"), 8 * i + k + 1)
                        tile_high(UP[0][:, k], U[:, k])

            def ffn(i):
                a, silu, base, s0 = sem("ffn_a"), sem("ffn_silu"), FT * i, split_at[f"ffn{i}"]

                def tile(j, r):
                    act.wait_ge(a, j + (base + 1))
                    dst = G[:, j] if isinstance(j, int) else G[:, bass.ds(j, 1)].rearrange("p a s -> p (a s)")
                    A_(dst, bank[2 * (r % 2)][:], ACT.Silu).then_inc(silu, 1)

                weights_high(s0 + 2)
                for j in range(2):
                    tile(j, j)
                weights_high(s0 + 3)
                with act.Fori(0, 3) as it:
                    for r in range(3):
                        more = it * (16 if i else 32)
                        weights_high(s0 + 4 + 2 * r, it * 6 + (base + 2 * r + 2), more)
                        for s in range(2):
                            tile(it * 6 + (2 + 2 * r + s), s)
                        weights_high(s0 + 5 + 2 * r, it * 6 + (base + 2 * r + 4), more)
                weights_high(s0 + 22)
                for j in range(20, 22):
                    tile(j, j)

                def ready(k):
                    act.wait_ge(sem("ffn_g"), base + k + 1)
                    if k == 0:
                        act.wait_ge(sem("ffn_b"), base + FT)

                out_high(f"ffn{i}_out", FT, lambda k: G[:, k], UP, ready)

            def to_tokens(n):
                if n < 2:
                    act.wait_ge(sem("h"), 32 + 16 * n)
                for g in range(8):
                    act.wait_ge(sem("xt_tp"), 8 * n + g + 1)
                    t, half = g // 2, g % 2
                    evac(XT[:, t, 512 * half:512 * half + 512], bank[g % 4][:], "xt")

            def moe(l):
                to_tokens(l)
                act.wait_ge(sem("moe_m"), l + 1)
                for t in range(TT):
                    A_(RK[:, 96 + 8 * t:104 + 8 * t], LG[:, t, 0:GROUPS], ACT.Exp, bias=RK[:, 64 + t:65 + t],
                       accum_out=RK[:, 68 + t:69 + t]).then_inc(sem("moe_ge"), 1)
                act.wait_ge(sem("moe_d"), l + 1)
                A_(RK[:, 76:80], RK[:, 72:76], ACT.Exp).then_inc(sem("moe_ee"), 1)
                for g in range(16):
                    act.wait_ge(sem("moe_gather"), 16 * l + g + 1)
                    c, k = g // 8, g % 8
                    evac(XST[:, k, 512 * c:512 * c + 512], bank[g % 4][:], "moe_xst")
                act.wait_ge(sem("moe_plan"), l + 1)
                n = act.value_load(plan[0:1, 1:2], min_val=EXPERTS // 2, max_val=MAX_ROUNDS * EXPERTS // 2)

                def gate_part(e, s):
                    act.wait_ge(sem(f"moe{l}_ab"), e + 1)
                    A_(SA[:, s], bank[s][:, 0:P], ACT.Silu).then_inc(sem(f"moe{l}_silu"), 1)

                def turned(e, s):
                    act.wait_ge(sem(f"moe{l}_tp"), e + 1)
                    evac(HM[:, s], bank[2 + s][:, 0:P], f"moe{l}_ht")

                gate_part(0, 0)
                with act.Fori(1, n) as i:
                    gate_part(i * 2 - 1, 1)
                    turned(i * 2 - 2, 0)
                    gate_part(i * 2, 0)
                    turned(i * 2 - 1, 1)
                but_last, last = ends(act)
                gate_part(last, 1)
                turned(but_last, 0)
                turned(last, 1)
                for g in range(16):
                    act.wait_ge(sem("moe_ystp"), 16 * l + g + 1)
                    evac(YS[:, g // 2, 512 * (g % 2):512 * (g % 2) + 512], bank[g % 4][:], "moe_ys")

            weights_high(0)
            weights_high(1)
            norm(0, 0, lambda k: mod[:, k:k + 1], True)
            ffn(0)
            norm(1, 0, lambda k: mod[:, 24 + k:25 + k])
            act.wait_ge(sem("angles"), 1)
            A_(sinT, TB[:, 2], ACT.Sin).then_inc(sem("tables"), 1)
            A_(cosT, TB[:, 4], ACT.Sin).then_inc(sem("tables"), 1)
            for m in range(42):
                act.wait_ge(sem("mix_tile"), m + 1)
                src = bank[m % 4][:]
                if m < 2:
                    evac(PB[:, m, 16:528], src, "mix_evac")
                elif m < 8:
                    act.wait_ge(sem("tables"), 2)
                    evac(Q[:, m - 2], src, "mix_evac")
                elif m < 14:
                    evac(K[:, m - 8], src, "mix_evac")
                elif m < 26:
                    evac(V[:, (m - 14) // 4, (m - 14) % 4], src[:, 0:256], "mix_evac")
                else:
                    A_(GT[:, m - 26], src, ACT.Sigmoid).then_inc(sem("mix_evac"), 1)
            for k in range(2):
                act.wait_ge(sem("yp_mm"), k + 1)
                A_(YP[:, k], bank[6 + k][:], ACT.Copy, scale=col("pool_scale", k)).then_inc(sem("yp"), 1)

            for i in range(16 + 2):
                if i < 16:
                    act.wait_ge(sem("att_max"), i + 1)
                    A_(S1[:, i % 3], S1[:, i % 3], ACT.Exp, bias=small[:, i:i + 1],
                       accum_out=small[:, 16 + i:17 + i]).then_inc(sem("att_e"), 1)
                if 0 <= i - 1 < 16:
                    u = i - 1
                    act.wait_ge(sem("att_ri"), u + 1)
                    A_(S1[:, u % 3], S1[:, u % 3], ACT.Copy, scale=small[:, 32 + u:33 + u]).then_inc(sem("att_p"), 1)
                if i >= 2:
                    u = i - 2
                    act.wait_ge(sem("att_tp"), u + 1)
                    if u >= 2:
                        act.wait_ge(sem("att_pv"), u - 1)
                    st.did(A_(PT1[:, u % 2, 0:512], bank[4][:], ACT.Copy))
                    A_(PT1[:, u % 2, 512:768], bank[5][:, 0:256], ACT.Copy).then_inc(sem("att_pt"), 1)
            act.wait_ge(sem("merged"), 8)
            out_high("mix_out", KT, lambda k: MG[:, k], UP_MIX, lambda k: None)
            weights_high(split_at["ffn1"])
            weights_high(split_at["ffn1"] + 1)
            norm(2, 0, lambda k: mod[:, 48 + k:49 + k], True)
            ffn(1)
            for i in range(2):
                weights_high(split_at["conv"] + i)
            norm(3, 0, lambda k: epsc[:, 2:3], True)
            weights_high(split_at["conv"] + 2)
            def conv_ready(k):
                act.wait_ge(sem("conv_bc"), k + 1)
                if k == 0:
                    act.wait_ge(sem("conv_b"), 8)

            for d in range(KT):
                act.wait_ge(sem("conv_c"), d + 1)
                if d >= 2:
                    act.wait_ge(sem("conv_u"), d - 1)
                evac(CG[:, d % 2], bank[3 * (d % 2)][:], "conv_cg")
                if d % 2:
                    for i in range(3 if d < 7 else 1):
                        weights_high(split_at["conv"] + 3 * (d // 2 + 1) + i)
            out_high("conv_out", KT, lambda k: BC[:, k], UP, lambda k: conv_ready(k))
            norm(4, 1, lambda k: col("ln1_b", k))
            moe(0)
            norm(5, 2, lambda k: col("ln2_b", k))
            for t in range(4):
                act.wait_ge(sem("qi_mm"), t + 1)
                evac(QI[:, t], bank[t][:], "qi")
            act.wait_ge(sem("var"), 1)
            A_(DS[:, 216:224], DS[:, 192:200], ACT.Sqrt).then_inc(sem("sdev"), 1)
            act.wait_ge(sem("kv_tp"), 1)
            evac(CKVT, bank[6][:], "kvt")
            act.wait_ge(sem("kv_tp"), 2)
            evac(KIT, bank[7][:], "kvt")
            m = 0
            for qb in range(1, TT):
                for h in range(IDX_HEADS):
                    act.wait_ge(sem("idx_mm"), m + 1)
                    if m >= 2:
                        act.wait_ge(sem("idx_acc"), m - 1)
                    A_(IR[:, m % 2, 0:(qb + 1) * P], bank[m % 4][:, 0:(qb + 1) * P], ACT.Relu,
                       scale=IDX_DIM ** -0.5).then_inc(sem("idx_relu"), 1)
                    m += 1
            for h in range(HEADS2):
                act.wait_ge(sem("dsa_q"), h + 1)
                evac(Q2[:, h], bank[4 + h % 4][:], "q2")
            units = [(qb, h) for qb in range(TT) for h in range(HEADS2)]
            for i in range(len(units) + 2):
                if i < len(units):
                    n = (units[i][0] + 1) * P
                    act.wait_ge(sem("ds_max"), i + 1)
                    A_(S2[:, i % 3, 0:n], S2[:, i % 3, 0:n], ACT.Exp, bias=DS[:, i:i + 1],
                       accum_out=DS[:, 64 + i:65 + i]).then_inc(sem("ds_e"), 1)
                if 0 <= i - 1 < len(units):
                    u = i - 1
                    n = (units[u][0] + 1) * P
                    act.wait_ge(sem("ds_ri"), u + 1)
                    A_(S2[:, u % 3, 0:n], S2[:, u % 3, 0:n], ACT.Copy, scale=DS[:, 128 + u:129 + u])\
                        .then_inc(sem("ds_p"), 1)
                if i >= 2:
                    u = i - 2
                    n = (units[u][0] + 1) * P
                    act.wait_ge(sem("ds_tp"), u + 1)
                    if u >= 2:
                        act.wait_ge(sem("ds_pv"), u - 1)
                    A_(PT2[:, u % 2, 0:n], bank[2 + u % 2][:, 0:n], ACT.Copy).then_inc(sem("ds_pt"), 1)
            act.wait_ge(sem("ds_o"), 64)
            out_high("dsa_out", HEADS2, lambda k: Q2[:, k], UP, lambda k: None)
            norm(6, 3, lambda k: col("ln1_b", 8 + k))
            moe(1)
            norm(7, 4, lambda k: col("ln2_b", 8 + k))
            to_tokens(2)

        @block.vector
        def _(dve):
            st = Steps(dve, sem("dve_step"))
            TSc, STT, TTn = nc.vector.tensor_scalar, nc.vector.scalar_tensor_tensor, nc.vector.tensor_tensor

            def seq(ins):
                st.did(ins)
                st.wait()

            dve.wait_ge(sem("par"), 16)
            dve.wait_ge(sem("csil"), 1)

            def ada(n, a, r, more=0):
                landed(dve, "a", n, more)
                if not isinstance(a, int) or a >= 2:
                    dve.wait_ge(sem("ada_mm"), a - 1)
                w = chunk("a", n)
                for k in range(KT):
                    acc = AC[:, r % 2, k % 2]
                    if k < 2:
                        i = TSc(acc, w[:, k], csil[:, k:k + 1], None, ALU.mult)
                    else:
                        if k % 2 == 0:
                            dve.wait_ge(sem("ada_step"), a * 8 + k)
                        i = STT(out=acc, in0=w[:, k], scalar=csil[:, k:k + 1], in1=acc, op0=ALU.mult, op1=ALU.add)
                    i.then_inc(sem("ada_step"), 1)

            def ada_mod(a, r):
                dve.wait_ge(sem("ada_mm"), a + 1)
                if isinstance(a, int):
                    dst, b = mod[:, 2 * a:2 * a + 2], par[:, PC["b_ada"] + 2 * a:PC["b_ada"] + 2 * a + 2]
                else:
                    dst, b = mod[:, bass.ds(a * 2, 2)], par[:, bass.ds(a * 2 + PC["b_ada"], 2)]
                TTn(dst, bank[4 + r % 2][:, 0:2 * P:P], b, ALU.add).then_inc(sem("ada_mod"), 1)

            def modulation(i):
                a = 24 * i
                g = PC[("g_ffn1", "g_mix", "g_ffn2")[i]]
                st.did(STT(out=gains[:, 8 * i:8 * i + 8], in0=mod[:, a + 8:a + 16], scalar=1.0,
                           in1=par[:, g:g + 8], op0=ALU.add, op1=ALU.mult))
                st.did(TSc(gates[:, 8 * i:8 * i + 8], mod[:, a + 16:a + 24], (0.5, 1.0, 0.5)[i], None, ALU.mult))

            for a in range(ADA_FIRST):
                ada(a, a, a)
                if a:
                    ada_mod(a - 1, a - 1)
            ada_mod(ADA_FIRST - 1, ADA_FIRST - 1)
            dve.wait_ge(sem("ada_mod"), ADA_FIRST)
            modulation(0)
            st.wait()

            def weights_low(i, j=None):
                dve.wait_ge(sem("w_high"), (i if j is None else j) + 1)
                n = splits[i][1] % RING
                buf, nk, cols = high(i)
                TTn(ring_low[:, n, 0:nk * cols], ring[:, n, 0:nk * cols], buf.bitcast(F32), ALU.subtract)\
                    .then_inc(sem("w_low"), 1)

            def tile_low(m, pair, at, src):
                dve.wait_ge(sem("t_high"), m + 1)
                TTn(pair[1][:, at], src, pair[0][:, at].bitcast(F32), ALU.subtract).then_inc(sem("t_low"), 1)

            def out_low(name, kts, rhs, pair):
                n = 2 * -(-kts // 4)
                m = tiles_at[name]
                for q in range(n):
                    if q or name == "dsa_out" or name == "mix_out":
                        weights_low(split_at[name] + q)
                    if kts > KT or q < n // 2:
                        k0 = 4 * (q % (n // 2))
                        for k in range(k0, min(k0 + 4, kts)):
                            tile_low(m, pair, 4 * (q % 2) + k - k0, rhs(k))
                            m += 1

            def u_low(name):
                for k in range(KT):
                    tile_low(tiles_at[name] + k, UP, k, U[:, k])

            def norm(i, ln, gain):
                if ln:
                    dve.wait_ge(sem("mean"), ln)
                    for k in range(KT):
                        STT(out=H[:, k], in0=bank[6][:], scalar=-1.0 / D, in1=H[:, k],
                            op0=ALU.mult, op1=ALU.add).then_inc(sem("centred"), 1)
                dve.wait_ge(sem("root"), i + 1)
                seq(nc.vector.reciprocal(rstd[:], rstd[:]))
                for k in range(KT):
                    STT(out=U[:, k], in0=H[:, k], scalar=gain(k), in1=rstd[:],
                        op0=ALU.mult, op1=ALU.mult).then_inc(sem("normed"), 1)

            def ffn(i):
                b, g, silu, base, s0 = sem("ffn_b"), sem("ffn_g"), sem("ffn_silu"), FT * i, split_at[f"ffn{i}"]

                def tile(j, r):
                    dve.wait_ge(silu, j + (base + 1))
                    dve.wait_ge(b, j + (base + 1))
                    dst = G[:, j] if isinstance(j, int) else G[:, bass.ds(j, 1)].rearrange("p a s -> p (a s)")
                    TTn(dst, bank[2 * (r % 2) + 1][:], dst, ALU.mult).then_inc(g, 1)

                def some_ada(c, it, which):
                    for m in which:
                        a = ada_of(c)[m]
                        now = a if it is None else it * 6 + a
                        ada(ffn_at(0, c) + 2 + m, now, a, 0 if it is None else it * 32)
                        if a > ADA_FIRST:
                            ada_mod(now - 1, a - 1)

                def pair(c, it, s_next):
                    now = None if it is None else it * 6
                    n = 3 if c in (0, 10) else 2
                    for s in range(2):
                        if i == 0:
                            some_ada(c, it, range(1, n) if s else range(1))
                        if s_next[s] is not None:
                            weights_low(s_next[s], None if it is None else it * 6 + s_next[s])
                        j = 2 * c + s
                        tile(j if it is None else it * 6 + j, s)

                pair(0, None, (s0 + 2, s0 + 3))
                with dve.Fori(0, 3) as it:
                    for r in range(3):
                        pair(1 + r, it, (s0 + 4 + 2 * r, s0 + 5 + 2 * r))
                pair(10, None, (s0 + 22, None))
                if i == 0:
                    ada_mod(ADA_ALL - 1, ADA_ALL - 1)
                    dve.wait_ge(sem("ada_mod"), ADA_ALL)
                    modulation(1)
                    modulation(2)
                    st.wait()
                out_low(f"ffn{i}_out", FT, lambda k: G[:, k], UP)

            def gated_add(name, n, gate):
                for half in range(2):
                    dve.wait_ge(sem(name + "_used"), n * (half + 1))
                    for d in range(4):
                        k = 4 * half + d
                        STT(out=H[:, k], in0=bank[k][:], scalar=gates[:, gate + k:gate + k + 1], in1=H[:, k],
                            op0=ALU.mult, op1=ALU.add).then_inc(sem("h"), 1)

            def deep_add(k, src):
                STT(out=H[:, k], in0=U[:, k], scalar=ALPHA, in1=src, op0=ALU.mult, op1=ALU.add)\
                    .then_inc(sem("h"), 1)

            weights_low(0)
            weights_low(1)
            norm(0, 0, lambda k: gains[:, k:k + 1])
            u_low("ffn0")
            ffn(0)
            gated_add("ffn0_out", 6, 0)
            dve.wait_ge(sem("mix_const"), 80)
            ang, k1, r1, r2 = TB[:, 0], TB[:, 1], TB[:, 2], TB[:, 4]
            big = 12582912.0
            seq(nc.vector.tensor_copy(ang, posi))
            seq(TSc(ang, ang, invf[:, 0:1], None, ALU.mult))
            seq(TSc(k1, ang, 1.0 / (2 * np.pi), big, ALU.mult, ALU.add))
            seq(TSc(k1, k1, big, None, ALU.subtract))
            c1 = 6.28125
            c2 = float(np.float32(np.round((2 * np.pi - c1) * 2 ** 22) / 2 ** 22))
            c3 = float(2 * np.pi - c1 - c2)
            seq(STT(out=r1, in0=k1, scalar=-c1, in1=ang, op0=ALU.mult, op1=ALU.add))
            seq(STT(out=r1, in0=k1, scalar=-c2, in1=r1, op0=ALU.mult, op1=ALU.add))
            seq(STT(out=r1, in0=k1, scalar=-c3, in1=r1, op0=ALU.mult, op1=ALU.add))
            top = 3.1415925
            seq(TSc(r2, r1, float(np.pi / 2), None, ALU.add))
            seq(TSc(TB[:, 3], r2, float(np.pi), float(-2 * np.pi), ALU.is_gt, ALU.mult))
            seq(TTn(r2, r2, TB[:, 3], ALU.add))
            seq(TSc(r2, r2, top, -top, ALU.min, ALU.max))
            TSc(r1, r1, top, -top, ALU.min, ALU.max).then_inc(sem("angles"), 1)
            norm(1, 0, lambda k: gains[:, 8 + k:9 + k])
            dve.wait_ge(sem("tables"), 2)
            for r in range(12):
                t = Q[:, r] if r < 6 else K[:, r - 6]
                dve.wait_ge(sem("rot"), r + 1)
                st.did(TTn(RT[:, 0], t, cosT, ALU.mult))
                st.did(TTn(RT[:, 1], bank[4 + r % 2][:], sinT, ALU.mult))
                st.wait()
                TTn(t, RT[:, 0], RT[:, 1], ALU.add).then_inc(sem("rope"), 1)
                dve.wait_ge(sem("rope"), r + 1)
            dve.wait_ge(sem("pool_d"), 1)
            dve.wait_ge(sem("yp"), 2)
            for i in range(16 + 3):
                if i < 16:
                    u = i
                    c = u % CLASSES
                    lo, hi = bank[2 * (u % 2)], bank[2 * (u % 2) + 1]
                    dve.wait_ge(sem("att_mm"), u + 1)
                    if u >= 3:
                        dve.wait_ge(sem("att_tp"), u - 2)
                    S = S1[:, u % 3]
                    st.did(STT(out=S[:, 0:512], in0=lo[:], scalar=HEAD ** -0.5, in1=band[:, c],
                               op0=ALU.mult, op1=ALU.add))
                    st.did(STT(out=S[:, 512:640], in0=hi[:, 0:P], scalar=HEAD ** -0.5, in1=causal,
                               op0=ALU.mult, op1=ALU.add))
                    STT(out=S[:, 640:768], in0=hi[:, P:2 * P], scalar=HEAD ** -0.5, in1=mod4,
                        op0=ALU.mult, op1=ALU.add).then_inc(sem("att_s"), 1)
                    st.wait()
                    dve.wait_ge(sem("att_s"), u + 1)
                    nc.vector.tensor_reduce(small[:, u:u + 1], S, AXX, ALU.max, negate=True)\
                        .then_inc(sem("att_max"), 1)
                if 0 <= i - 1 < 16:
                    u = i - 1
                    dve.wait_ge(sem("att_e"), u + 1)
                    nc.vector.reciprocal(small[:, 32 + u:33 + u], small[:, 16 + u:17 + u]).then_inc(sem("att_ri"), 1)
                if i >= 3:
                    u = i - 3
                    h, c = u // CLASSES, u % CLASSES
                    r = 64 * (h % 2)
                    dve.wait_ge(sem("att_pv"), u + 1)
                    nc.vector.tensor_copy(YA[r:r + 64, h // 2, c:SEQ:CLASSES], bank[6 + u % 2][r:r + 64, 0:P])\
                        .then_inc(sem("att_y"), 1)
            dve.wait_ge(sem("att_y"), 16)
            for d in range(KT):
                dve.wait_ge(sem("merge_ab"), d + 1)
                st.did(TTn(MG[:, d], bank[(2 * d) % 4][:], GT[:, d], ALU.mult))
                st.did(TTn(RT2[:], bank[(2 * d + 1) % 4][:], GT[:, 8 + d], ALU.mult))
                st.wait()
                TTn(MG[:, d], MG[:, d], RT2[:], ALU.add).then_inc(sem("merged"), 1)
                dve.wait_ge(sem("merged"), d + 1)
            out_low("mix_out", KT, lambda k: MG[:, k], UP_MIX)
            gated_add("mix_out", 2, 8)
            for i in range(2):
                weights_low(split_at["ffn1"] + i)
            norm(2, 0, lambda k: gains[:, 16 + k:17 + k])
            u_low("ffn1")
            ffn(1)
            gated_add("ffn1_out", 6, 16)
            for i in range(2):
                weights_low(split_at["conv"] + i)
            norm(3, 0, lambda k: col("g_final", k))
            u_low("conv")
            weights_low(split_at["conv"] + 2)
            st.did(nc.vector.memset(CU[:, :, 0:2], 0.0))
            st.wait()
            for d in range(KT):
                b3 = 3 * (d % 2)
                cu, cv = CU[:, d % 2], CV[:, d % 2]
                dve.wait_ge(sem("conv_cg"), d + 1)
                dve.wait_ge(sem("conv_h"), d + 1)
                TTn(cu[:, 2:SEQ + 2], bank[b3 + 1][:], CG[:, d % 2], ALU.mult).then_inc(sem("conv_u"), 1)
                dve.wait_ge(sem("conv_u"), d + 1)
                seq(TSc(cv, cu[:, 0:SEQ], col("conv_k", d), None, ALU.mult))
                seq(STT(out=cv, in0=cu[:, 1:SEQ + 1], scalar=col("conv_k", 8 + d), in1=cv, op0=ALU.mult, op1=ALU.add))
                seq(STT(out=cv, in0=cu[:, 2:SEQ + 2], scalar=col("conv_k", 16 + d), in1=cv, op0=ALU.mult, op1=ALU.add))
                if d % 2:
                    for i in range(2 if d < 7 else 1):
                        weights_low(split_at["conv"] + 3 * (d // 2 + 1) + i)
                dve.wait_ge(sem("conv_b"), d + 1)
                TTn(BC[:, d], bank[b3 + 2][:], cv, ALU.mult).then_inc(sem("conv_bc"), 1)
                if d % 2 and d < 7:
                    weights_low(split_at["conv"] + 3 * (d // 2 + 1) + 2)
            out_low("conv_out", KT, lambda k: BC[:, k], UP)

            def deep_out(name, n):
                for half in range(2):
                    dve.wait_ge(sem(name + "_used"), n * (half + 1))
                    for d in range(4):
                        deep_add(4 * half + d, bank[4 * half + d][:])

            deep_out("conv_out", 2)
            norm(4, 1, lambda k: col("ln1_g", k))

            def moe(l):
                dve.wait_ge(sem("rows"), 16 * 11)
                T4 = range(TT)
                r = RK
                top, idx = r[:, 0:32], r[:, 32:64].bitcast(U32)
                negm, gden, dif, ex = r[:, 64:68], r[:, 68:72], r[:, 72:76], r[:, 76:80]
                gi, w0, w1, id0, id1 = r[:, 80:84], r[:, 84:88], r[:, 88:92], r[:, 92:96], r[:, 128:132]
                d0, d1 = r[:, 132:136], r[:, 136:140]
                cnt, cum, one64 = r[:, 144:208], r[:, 208:272], r[:, 272:336]
                el, oh = r[:, 336:368], r[:, 368:400]
                etop, eidx = r[:, 400:432], r[:, 432:464].bitcast(U32)
                E0, E1, EA, RN = r[:, 512:768], r[:, 768:1024], r[:, 1024:1280], r[:, 1280:1536]
                tmp = r[:, 1536:1792]
                cell = lambda v, t, n: v[:, n * t:n * t + n]
                dve.wait_ge(sem("moe_logits"), l + 1)
                for t in T4:
                    st.did(TTn(LG[:, t], bank[4][:, 72 * t:72 * t + 72], rbias[:, l], ALU.add))
                st.wait()
                for t in T4:
                    st.did(nc.vector.max(cell(top, t, 8), LG[:, t, 0:GROUPS]))
                st.wait()
                for t in T4:
                    st.did(TSc(cell(negm, t, 1), top[:, 8 * t:8 * t + 1], -1.0, None, ALU.mult))
                    st.did(nc.vector.max_index(cell(idx, t, 8), cell(top, t, 8), LG[:, t, 0:GROUPS]))
                st.wait()
                for t in T4:
                    i = nc.vector.tensor_copy(cell(gi, t, 1), idx[:, 8 * t:8 * t + 1])
                    i.then_inc(sem("moe_m"), 1) if t == TT - 1 else st.did(i)
                st.wait()
                dve.wait_ge(sem("moe_m"), l + 1)
                for t in T4:
                    st.did(TSc(cell(oh, t, 8), lane[:, 0:8], cell(gi, t, 1), None, ALU.is_equal))
                st.wait()
                for g in range(GROUPS):
                    for t in T4:
                        src = LG[:, t, 8 + 8 * g:16 + 8 * g]
                        o = oh[:, 8 * t + g:8 * t + g + 1]
                        if g == 0:
                            st.did(TSc(cell(el, t, 8), src, o, None, ALU.mult))
                        else:
                            st.did(STT(out=cell(el, t, 8), in0=src, scalar=o, in1=cell(el, t, 8),
                                       op0=ALU.mult, op1=ALU.add))
                    st.wait()
                for t in T4:
                    st.did(nc.vector.max(cell(etop, t, 8), cell(el, t, 8)))
                st.wait()
                for t in T4:
                    st.did(nc.vector.max_index(cell(eidx, t, 8), cell(etop, t, 8), cell(el, t, 8)))
                    i = TTn(cell(dif, t, 1), etop[:, 8 * t + 1:8 * t + 2], etop[:, 8 * t:8 * t + 1], ALU.subtract)
                    i.then_inc(sem("moe_d"), 1) if t == TT - 1 else st.did(i)
                st.wait()
                for t in T4:
                    st.did(nc.vector.tensor_copy(cell(id0, t, 1), eidx[:, 8 * t:8 * t + 1]))
                    st.did(nc.vector.tensor_copy(cell(id1, t, 1), eidx[:, 8 * t + 1:8 * t + 2]))
                st.wait()
                for i in (id0, id1):
                    st.did(STT(out=i, in0=gi, scalar=float(PER_GROUP), in1=i, op0=ALU.mult, op1=ALU.add))
                st.wait()
                for t in T4:
                    st.did(TSc(cell(E0, t, 64), lane[:, 0:64], cell(id0, t, 1), None, ALU.is_equal))
                    st.did(TSc(cell(E1, t, 64), lane[:, 0:64], cell(id1, t, 1), None, ALU.is_equal))
                st.wait()
                TTn(EA, E0, E1, ALU.add).then_inc(sem("moe_ea"), 1)
                dve.wait_ge(sem("moe_ge"), 4 * l + 4)
                dve.wait_ge(sem("moe_ee"), l + 1)
                seq(STT(out=w0, in0=ex, scalar=1.0, in1=gden, op0=ALU.add, op1=ALU.mult))
                seq(nc.vector.reciprocal(w0, w0))
                st.did(TTn(w1, w0, ex, ALU.mult))
                dve.wait_ge(sem("moe_rank"), l + 1)
                st.did(nc.vector.tensor_copy(cnt, bank[5][:, 256:320]))
                st.did(nc.vector.memset(one64, 1.0))
                st.wait()
                seq(nc.vector.tensor_tensor_scan(cum, one64, cnt, 0.0, ALU.mult, ALU.add))
                seq(TTn(startf, cum, cnt, ALU.subtract))
                for t in T4:
                    st.did(TTn(cell(RN, t, 64), bank[5][:, 64 * t:64 * t + 64], startf, ALU.add))
                st.wait()
                for t in T4:
                    for E, d in ((E0, d0), (E1, d1)):
                        seq(nc.vector.tensor_tensor_reduce(tmp[:, 0:64], cell(E, t, 64), cell(RN, t, 64), 1.0, 0.0,
                                                           ALU.mult, ALU.add, cell(d, t, 1)))
                for j in range(MAX_ROUNDS):
                    st.did(TSc(REM[:, 64 * j:64 * j + 64], cnt, lanecol, float(WIN * j), ALU.subtract, ALU.is_gt))
                    st.did(TSc(STI[:, 64 * j:64 * j + 64], startf, float(WIN * j), float(PAIRS), ALU.add, ALU.min))
                seq(nc.vector.tensor_reduce(tmp[:, 0:1], cnt, AXX, ALU.max))
                seq(TSc(plan[:, 2:3], tmp[:, 0:1], float(WIN - 1), None, ALU.add))
                seq(TSc(plan[:, 0:1], plan[:, 2:3], 6, None, ALU.arith_shift_right))
                st.did(TSc(plan[:, 3:4], plan[:, 0:1], 6, None, ALU.logical_shift_left))
                st.wait()
                st.did(TSc(plan[:, 2:3], plan[:, 3:4], 1.0, None, ALU.subtract))
                seq(TSc(plan[:, 4:5], plan[:, 3:4], 2.0, None, ALU.subtract))
                TSc(plan[:, 1:2], plan[:, 0:1], 5, None, ALU.logical_shift_left).then_inc(sem("moe_plan"), 1)
                for t in T4:
                    seq(TSc(SELW[:, t], slotrow, cell(d0, t, 1), None, ALU.is_equal))
                    STT(out=SEL[:, t], in0=slotrow, scalar=cell(d1, t, 1), in1=SELW[:, t],
                        op0=ALU.is_equal, op1=ALU.add).then_inc(sem("moe_sel"), 1)
                for t in T4:
                    dve.wait_ge(sem("moe_sel"), 4 * l + t + 1)
                nc.vector.memset(XST[:, :, PAIRS:SLOTS], 0.0).then_inc(sem("moe_tail"), 1)
                for t in T4:
                    seq(TSc(SELT, slotrow, cell(d1, t, 1), cell(w1, t, 1), ALU.is_equal, ALU.mult))
                    seq(STT(out=SELW[:, t], in0=SELW[:, t], scalar=cell(w0, t, 1), in1=SELT,
                            op0=ALU.mult, op1=ALU.add))
                dve.wait_ge(sem("moe_gather"), 16 * l + 16)
                nc.vector.memset(YST, 0.0).then_inc(sem(f"moe{l}_add"), 1)
                dve.wait_ge(sem("moe_plan"), l + 1)
                n = dve.value_load(plan[0:1, 1:2], min_val=EXPERTS // 2, max_val=MAX_ROUNDS * EXPERTS // 2)

                def hidden(e, s):
                    dve.wait_ge(sem(f"moe{l}_silu"), e + 1)
                    m = REM[:, e:e + 1] if isinstance(e, int) else REM[:, bass.ds(e, 1)]
                    STT(out=HB[:, s], in0=SA[:, s], scalar=m, in1=bank[s][:, P:2 * P],
                        op0=ALU.mult, op1=ALU.mult).then_inc(sem(f"moe{l}_h"), 1)

                def collect(e, s):
                    at = dve.value_load(STI[0:1, bass.ds(e, 1)], min_val=0, max_val=PAIRS)
                    dve.wait_ge(sem(f"moe{l}_y"), e + 1)
                    dve.wait_ge(sem(f"moe{l}_add"), e + 1)
                    w = YST[:, :, bass.ds(at, WIN)]
                    TTn(w, bank[4 + s][:].rearrange("p (k n) -> p k n", k=KT), w, ALU.add)\
                        .then_inc(sem(f"moe{l}_add"), 1)

                hidden(0, 0)
                with dve.Fori(1, n) as i:
                    hidden(i * 2 - 1, 1)
                    collect(i * 2 - 2, 0)
                    hidden(i * 2, 0)
                    collect(i * 2 - 1, 1)
                but_last, last = ends(dve)
                hidden(last, 1)
                collect(but_last, 0)
                collect(last, 1)
                for g in range(8):
                    dve.wait_ge(sem("moe_swtp"), 8 * l + g + 1)
                    nc.vector.tensor_copy(SWT[:, g], bank[4 + g % 4][:]).then_inc(sem("moe_swt"), 1)
                for d in range(KT):
                    dve.wait_ge(sem("moe_f"), 8 * l + d + 1)
                    deep_add(d, bank[d % 4][:])

            moe(0)
            norm(5, 2, lambda k: col("ln2_g", k))

            dve.wait_ge(sem("vb_mm"), 1)
            nc.vector.tensor_copy(VB[0:HEADS2, 0:512], bank[6][0:HEADS2, :]).then_inc(sem("vb"), 1)
            nc.vector.tensor_copy(VB[0:HEADS2, 512:640], bank[7][0:HEADS2, 0:P]).then_inc(sem("vb"), 1)
            dve.wait_ge(sem("kv_mm"), 1)
            sq = S2
            for t in range(TT):
                src = bank[4][:, P * t:P * t + P]
                st.did(nc.vector.tensor_copy(CKV[:, t], src))
            st.wait()
            for t in range(TT):
                seq(nc.vector.tensor_tensor_reduce(S2[:, 0, 0:P], CKV[:, t], CKV[:, t], 1.0, 0.0,
                                                   ALU.mult, ALU.add, DS[:, 192 + t:193 + t]))
            seq(TSc(DS[:, 192:196], DS[:, 192:196], 1.0 / LATENT, RMS_EPS, ALU.mult, ALU.add))
            dve.wait_ge(sem("ki_mm"), 1)
            for t in range(TT):
                st.did(nc.vector.tensor_copy(KI[:, t, 0:64], bank[5][:, 72 * t:72 * t + 64]))
                st.did(TSc(W8[:, t], bank[5][:, 72 * t + 64:72 * t + 72], IDX_HEADS ** -0.5, None, ALU.mult))
            st.wait()
            for t in range(TT):
                st.did(nc.vector.tensor_reduce(DS[:, 200 + t:201 + t], KI[:, t, 0:64], AXX, ALU.add))
            st.wait()
            seq(TSc(DS[:, 200:204], DS[:, 200:204], 1.0 / IDX_DIM, None, ALU.mult))
            for t in range(TT):
                st.did(TSc(KI[:, t, 0:64], KI[:, t, 0:64], DS[:, 200 + t:201 + t], None, ALU.subtract))
            st.wait()
            for t in range(TT):
                seq(nc.vector.tensor_tensor_reduce(S2[:, 0, 0:64], KI[:, t, 0:64], KI[:, t, 0:64], 1.0, 0.0,
                                                   ALU.mult, ALU.add, DS[:, 196 + t:197 + t]))
            seq(TSc(DS[:, 196:200], DS[:, 196:200], 1.0 / IDX_DIM, LN_EPS, ALU.mult, ALU.add))
            nc.vector.tensor_copy(DS[:, 204:205], DS[:, 196:197]).then_inc(sem("var"), 1)
            dve.wait_ge(sem("sdev"), 1)
            seq(nc.vector.reciprocal(DS[:, 208:216], DS[:, 216:224]))
            for t in range(TT):
                STT(out=CKV[:, t], in0=CKV[:, t], scalar=DS[:, 208 + t:209 + t], in1=kvg[:],
                    op0=ALU.mult, op1=ALU.mult).then_inc(sem("ckv"), 1)
            for t in range(TT):
                st.did(STT(out=KI[:, t, 0:64], in0=KI[:, t, 0:64], scalar=DS[:, 212 + t:213 + t], in1=lng[:],
                           op0=ALU.mult, op1=ALU.mult))
            st.wait()
            for t in range(TT):
                st.did(TTn(KI[:, t, 64:128], KI[:, t, 0:64], lnb[:], ALU.add))
            st.wait()
            for t in range(TT):
                nc.vector.tensor_copy(KI[:, t, 0:64], KI[:, t, 64:128]).then_inc(sem("ki"), 1)
            m = 0
            for qb in range(1, TT):
                n = (qb + 1) * P
                acc = SM[:, qb - 1, 0:n]
                for h in range(IDX_HEADS):
                    dve.wait_ge(sem("idx_relu"), m + 1)
                    w = W8[:, qb, h:h + 1]
                    if h == 0:
                        TSc(acc, IR[:, m % 2, 0:n], w, None, ALU.mult).then_inc(sem("idx_acc"), 1)
                    else:
                        STT(out=acc, in0=IR[:, m % 2, 0:n], scalar=w, in1=acc, op0=ALU.mult, op1=ALU.add)\
                            .then_inc(sem("idx_acc"), 1)
                    m += 1
                    dve.wait_ge(sem("idx_acc"), m)
                st.did(TTn(acc[:, n - P:n], acc[:, n - P:n], causal, ALU.add))
            st.wait()
            for r in range(TOPK // 8):
                for qb in range(1, TT):
                    acc = SM[:, qb - 1, 0:(qb + 1) * P]
                    st.did(nc.vector.max(DS[:, 224 + 8 * qb:232 + 8 * qb], acc))
                st.wait()
                for qb in range(1, TT):
                    acc = SM[:, qb - 1, 0:(qb + 1) * P]
                    st.did(nc.vector.match_replace(acc, DS[:, 224 + 8 * qb:232 + 8 * qb], acc, TAKEN))
                st.wait()
            for qb in range(1, TT):
                acc = SM[:, qb - 1, 0:(qb + 1) * P]
                st.did(TSc(acc, acc, TAKEN / 2, NEG, ALU.is_gt, ALU.mult))
            st.wait()
            units = [(qb, h) for qb in range(TT) for h in range(HEADS2)]
            dve.wait_ge(sem("toe"), 16)

            for i in range(len(units) + 3):
                if i < len(units):
                    qb, h = units[i]
                    n = (qb + 1) * P
                    S = S2[:, i % 3, 0:n]
                    dve.wait_ge(sem("ds_mm"), i + 1)
                    if i >= 3:
                        dve.wait_ge(sem("ds_tp"), i - 2)
                    STT(out=S, in0=bank[i % 2][:, 0:n], scalar=LATENT ** -0.5, in1=TOE[:, h, SEQ - n:SEQ],
                        op0=ALU.mult, op1=ALU.add).then_inc(sem("ds_s"), 1)
                    dve.wait_ge(sem("ds_s"), i + 1)
                    seq(TTn(S, S, causal if qb == 0 else SM[:, qb - 1, 0:n], ALU.add))
                    nc.vector.tensor_reduce(DS[:, i:i + 1], S, AXX, ALU.max, negate=True).then_inc(sem("ds_max"), 1)
                if 0 <= i - 1 < len(units):
                    u = i - 1
                    dve.wait_ge(sem("ds_e"), u + 1)
                    nc.vector.reciprocal(DS[:, 128 + u:129 + u], DS[:, 64 + u:65 + u]).then_inc(sem("ds_ri"), 1)
                if i >= 3:
                    u = i - 3
                    qb, h = units[u]
                    dve.wait_ge(sem("ds_pv"), u + 1)
                    nc.vector.tensor_copy(Q2[:, h, qb * P:qb * P + P], bank[4 + u % 2][:, 0:P])\
                        .then_inc(sem("ds_o"), 1)
            out_low("dsa_out", HEADS2, lambda k: Q2[:, k], UP)
            deep_out("dsa_out", 4)
            norm(6, 3, lambda k: col("ln1_g", 8 + k))
            moe(1)
            norm(7, 4, lambda k: col("ln2_g", 8 + k))

        @block.tensor
        def _(pe):
            mm, tp = nc.tensor.matmul, nc.tensor.transpose
            pe.wait_ge(sem("x_in"), 16)
            pe.wait_ge(sem("keep"), 16)
            for k in range(KT):
                if k >= 4:
                    pe.wait_ge(sem("x_h"), k - 3)
                for t in range(TT):
                    i = tp(bank[k % 4][:, P * t:P * t + P], xtok[:, t, P * k:P * k + P], ident)
                i.then_inc(sem("x_tp"), 1)
            pe.wait_ge(sem("pool_step"), 1)

            def ada(a, r):
                pe.wait_ge(sem("ada_step"), a * 8 + 8)
                if not isinstance(a, int) or a >= 2:
                    pe.wait_ge(sem("ada_mod"), a - 1)
                for j in range(2):
                    for k in range(2):
                        x = mm(bank[4 + r % 2][:, P * j:P * j + P], AC[:, r % 2, k, P * j:P * j + P], ones[:],
                               start=(k == 0), stop=(k == 1))
                x.then_inc(sem("ada_mm"), 1)

            for a in range(ADA_FIRST):
                ada(a, a)

            def norm(i, ln):
                if ln:
                    pe.wait_ge(sem("h"), 8 * (i))
                    for k in range(KT):
                        x = mm(bank[6][:], ones[:], H[:, k], start=(k == 0), stop=(k == KT - 1))
                    x.then_inc(sem("mean"), 1)
                for k in range(KT):
                    pe.wait_ge(sem("squares"), 8 * i + k + 1)
                    x = mm(bank[7][:], ones[:], U[:, k], start=(k == 0), stop=(k == KT - 1))
                x.then_inc(sem("sumsq"), 1)

            def passes(o, w, cols, x, first_, last_):
                for n, (a, b) in enumerate(((w[0], x[0]), (w[0], x[1]), (w[1], x[0]))):
                    i = mm(o, a[:, cols[0], cols[1]], b,
                           start=first_ and n == 0, stop=last_ and n == 2)
                return i

            def ffn(i):
                a, b, g, base, s0 = sem("ffn_a"), sem("ffn_b"), sem("ffn_g"), FT * i, split_at[f"ffn{i}"]

                def pair(c, r, it):
                    for s in range(2):
                        if it is not None or r > 0:
                            pe.wait_ge(g, c * 2 + (base + s - 1))
                        for which, sm in enumerate((a, b)):
                            if s == 0:
                                pe.wait_ge(sem("w_low"), c * 2 + (s0 + which + 1))
                            w = both(s0 + 2 * r + which)
                            for k in range(KT):
                                if it is None and r == s == which == 0:
                                    pe.wait_ge(sem("t_low"), tiles_at[f"ffn{i}"] + k + 1)
                                x = passes(bank[2 * s + which][:], w, (k, slice(P * s, P * s + P)),
                                           (UP[0][:, k], UP[1][:, k]), k == 0, k == KT - 1)
                            x.then_inc(sm, 1)
                        if i == 0:
                            for a_ in (ada_of(r)[1:] if s else ada_of(r)[:1]):
                                ada(a_ if it is None else it * 6 + a_, a_)

                pair(0, 0, None)
                with pe.Fori(0, 3) as it:
                    for r in range(3):
                        pair(it * 3 + (1 + r), 1 + r, it)
                pair(10, 10, None)
                pe.wait_ge(g, base + FT)
                if i == 0:
                    pe.wait_ge(sem("ada_mod"), ADA_ALL)
                outproj(f"ffn{i}_out", FT, UP)

            def outproj(name, kts, x):
                i, t = split_at[name], tiles_at[name]
                q = 0
                for half in range(2):
                    for k0 in range(0, kts, 4):
                        pe.wait_ge(sem("w_low"), i + q + 1)
                        w = both(i + q)
                        for k in range(k0, min(k0 + 4, kts)):
                            m = k + (half * kts if kts > KT else 0)
                            pe.wait_ge(sem("t_low"), t + m + 1)
                            at = 4 * (q % 2) + k - k0
                            for d in range(4):
                                last = passes(bank[4 * half + d][:], w, (k - k0, slice(P * d, P * d + P)),
                                              (x[0][:, at], x[1][:, at]), k == 0, k == kts - 1)
                        last.then_inc(sem(name + "_used"), 1)
                        q += 1

            norm(0, 0)
            ffn(0)
            norm(1, 0)
            pe.wait_ge(sem("u"), 16)
            n0 = first["mix"]

            def rot(r):
                pe.wait_ge(sem("mix_evac"), r + 3)
                if r >= 2:
                    pe.wait_ge(sem("rope"), r - 1)
                src = Q[:, r] if r < 6 else K[:, r - 6]
                mm(bank[4 + r % 2][:], rotm, src, start=True, stop=True).then_inc(sem("rot"), 1)

            pe.wait_ge(sem("mix_const"), 80)
            m = 0
            for c in range(18):
                landed(pe, "a", n0 + c)
                w = chunk("a", n0 + c)
                if 7 <= c < 10:
                    for t in range(TT):
                        pe.wait_ge(sem("mix_evac"), m - 3)
                        for k in range(KT):
                            lhs = U[:, k, P * t:P * t + P] if c == 7 else U[:, k, t:SEQ:CLASSES]
                            x = mm(bank[m % 4][:, 0:256], lhs, w[:, k, :], start=(k == 0), stop=(k == KT - 1))
                        x.then_inc(sem("mix_tile"), 1)
                        m += 1
                        r = m - 5
                        if 0 <= r < 12:
                            rot(r)
                    continue
                for j in range(2):
                    if m >= 4:
                        pe.wait_ge(sem("mix_evac"), m - 3)
                    for k in range(KT):
                        x = mm(bank[m % 4][:], w[:, k, P * j:P * j + P], U[:, k], start=(k == 0), stop=(k == KT - 1))
                    x.then_inc(sem("mix_tile"), 1)
                    m += 1
                    r = m - 5
                    if 0 <= r < 12:
                        rot(r)
            pe.wait_ge(sem("pool_d"), 1)
            pe.wait_ge(sem("wpool"), 64)
            for k in range(2):
                mm(bank[6 + k][:], wpool[:, k], PD[:, k], start=True, stop=True).then_inc(sem("yp_mm"), 1)

            def scores(u):
                h, c = u // CLASSES, u % CLASSES
                r = 64 * (h % 2)
                R = slice(r, r + 64)
                lo, hi = bank[2 * (u % 2)], bank[2 * (u % 2) + 1]
                if u >= 2:
                    pe.wait_ge(sem("att_s"), u - 1)
                q = lambda g: Q[R, 2 * g + h // 2, c:SEQ:CLASSES]
                k = lambda g: K[R, 2 * g + h // 2, c:SEQ:CLASSES]
                mm(lo[:], q(0), K[R, h // 2, :], start=True, stop=True)
                mm(hi[:, 0:P], q(1), k(1), start=True, stop=True)
                mm(hi[:, P:2 * P], q(2), k(2), start=True, stop=True).then_inc(sem("att_mm"), 1)

            pe.wait_ge(sem("mix_evac"), 42)
            pe.wait_ge(sem("rope"), 12)
            pe.wait_ge(sem("yp"), 2)
            for i in range(16 + 3):
                if i < 16:
                    scores(i)
                if 0 <= i - 2 < 16:
                    u = i - 2
                    pe.wait_ge(sem("att_p"), u + 1)
                    if u:
                        pe.wait_ge(sem("att_pt"), u)
                    for j in range(6):
                        dst = bank[4][:, P * j:P * j + P] if j < 4 else bank[5][:, P * (j - 4):P * (j - 3)]
                        x = tp(dst, S1[:, u % 3, P * j:P * j + P], ident)
                    x.then_inc(sem("att_tp"), 1)
                if i >= 3:
                    u = i - 3
                    h, c = u // CLASSES, u % CLASSES
                    r = 64 * (h % 2)
                    pe.wait_ge(sem("att_pt"), u + 1)
                    if u >= 2:
                        pe.wait_ge(sem("att_y"), u - 1)
                    for j in range(6):
                        v = V[:, 0, j] if j < 4 else V[:, j - 3, c]
                        x = mm(bank[6 + u % 2][r:r + 64, 0:P], v[:, 64 * h:64 * h + 64], PT1[:, u % 2, P * j:P * j + P],
                               start=(j == 0), stop=(j == 5))
                    x.then_inc(sem("att_pv"), 1)
            n = first["branch"]
            landed(pe, "a", n)
            landed(pe, "a", n + 1)
            pe.wait_ge(sem("att_y"), 16)
            pe.wait_ge(sem("att_s"), 16)
            for d in range(KT):
                if d >= 2:
                    pe.wait_ge(sem("merged"), d - 1)
                for b, y in enumerate((YP, YA)):
                    for k in range(2):
                        x = mm(bank[(2 * d + b) % 4][:], chunk("a", n + b)[:, k, P * d:P * d + P], y[:, k],
                               start=(k == 0), stop=(k == 1))
                x.then_inc(sem("merge_ab"), 1)
            pe.wait_ge(sem("merged"), 8)
            outproj("mix_out", KT, UP_MIX)
            norm(2, 0)
            ffn(1)
            norm(3, 0)
            for j in range(4):
                for s in range(2):
                    d = 2 * j + s
                    if d >= 2:
                        pe.wait_ge(sem("conv_bc"), d - 1)
                    for which in range(3):
                        n = split_at["conv"] + 3 * j + which
                        pe.wait_ge(sem("w_low"), n + 1)
                        w = both(n)
                        for k in range(KT):
                            if d == which == 0:
                                pe.wait_ge(sem("t_low"), tiles_at["conv"] + k + 1)
                            x = passes(bank[3 * s + which][:], w, (k, slice(P * s, P * s + P)),
                                       (UP[0][:, k], UP[1][:, k]), k == 0, k == KT - 1)
                        x.then_inc(sem(("conv_c", "conv_h", "conv_b")[which]), 1)
            pe.wait_ge(sem("conv_bc"), 8)
            outproj("conv_out", KT, UP)
            norm(4, 1)

            def to_tokens(n, ready):
                pe.wait_ge(sem("u"), ready)
                for g in range(8):
                    if g >= 4:
                        pe.wait_ge(sem("xt"), 8 * n + g - 3)
                    t, half = g // 2, g % 2
                    for k in range(4):
                        x = tp(bank[g % 4][:, P * k:P * k + P], U[:, 4 * half + k, P * t:P * t + P], ident)
                    x.then_inc(sem("xt_tp"), 1)

            def moe(l):
                to_tokens(l, 40 + 16 * l)
                pe.wait_ge(sem("rows"), 16 * 11)
                for t in range(TT):
                    for k in range(KT):
                        x = mm(bank[4][:, 72 * t:72 * t + 72], U[:, k, P * t:P * t + P], rw[:, l, k],
                               start=(k == 0), stop=(k == KT - 1))
                x.then_inc(sem("moe_logits"), 1)
                EA = RK[:, 1024:1280]
                pe.wait_ge(sem("moe_ea"), l + 1)
                for t in range(TT):
                    for j in range(t + 1):
                        mm(bank[5][:, 64 * t:64 * t + 64], before if j == t else ones[:], EA[:, 64 * j:64 * j + 64],
                           start=(j == 0), stop=(j == t))
                for j in range(TT):
                    x = mm(bank[5][:, 256:320], ones[:], EA[:, 64 * j:64 * j + 64], start=(j == 0), stop=(j == 3))
                x.then_inc(sem("moe_rank"), 1)
                pe.wait_ge(sem("moe_sel"), 4 * l + 4)
                pe.wait_ge(sem("xt"), 8 * l + 8)
                for g in range(16):
                    c, k = g // 8, g % 8
                    if g >= 4:
                        pe.wait_ge(sem("moe_xst"), 16 * l + g - 3)
                    for t in range(TT):
                        x = mm(bank[g % 4][:], XT[:, t, P * k:P * k + P], SEL[:, t, 512 * c:512 * c + 512],
                               start=(t == 0), stop=(t == TT - 1))
                    x.then_inc(sem("moe_gather"), 1)
                pe.wait_ge(sem("moe_xst"), 16 * l + 16)
                pe.wait_ge(sem("moe_plan"), l + 1)
                n = pe.value_load(plan[0:1, 1:2], min_val=EXPERTS // 2, max_val=MAX_ROUNDS * EXPERTS // 2)

                def up(e, landed16, s):
                    pe.wait_ge(sem(f"moe{l}_xw"), e + 1)
                    for which in range(2):
                        pe.wait_ge(sem(f"w_m{l}{3 * s + which}"), landed16)
                    for k in range(KT):
                        for f in range(2):
                            c0 = D_EXP * k + P * f
                            x = mm(bank[s][64 * f:64 * f + 64, 0:2 * P].rearrange("p (w n) -> p w n", w=2),
                                   XW[:, s, k], ring[:, 3 * s:3 * s + 2, c0:c0 + P],
                                   start=(k == 0), stop=(k == KT - 1))
                    x.then_inc(sem(f"moe{l}_ab"), 1)

                def down(e, landed16, s):
                    pe.wait_ge(sem(f"moe{l}_h"), e + 1)
                    tp(bank[2 + s][:, 0:P], HB[:, s], ident).then_inc(sem(f"moe{l}_tp"), 1)
                    pe.wait_ge(sem(f"moe{l}_ht"), e + 1)
                    pe.wait_ge(sem(f"moe{l}_add"), e)
                    pe.wait_ge(sem(f"w_m{l}{3 * s + 2}"), landed16)
                    w = wview(3 * s + 2, 2, D)
                    for r in (0, 64):
                        for d in range(KT):
                            for f in range(2):
                                x = mm(bank[4 + s][r:r + 64, WIN * d:WIN * d + WIN],
                                       w[:, f, P * d + r:P * d + r + 64], HM[:, s, WIN * f:WIN * f + WIN],
                                       start=(f == 0), stop=(f == 1))
                    x.then_inc(sem(f"moe{l}_y"), 1)

                up(0, 16, 0)
                with pe.Fori(1, n) as i:
                    up(i * 2 - 1, i * 16, 1)
                    down(i * 2 - 2, i * 16, 0)
                    up(i * 2, i * 16 + 16, 0)
                    down(i * 2 - 1, i * 16, 1)
                but_last, last = ends(pe)
                up(last, n * 16, 1)
                down(but_last, n * 16, 0)
                down(last, n * 16, 1)
                pe.wait_ge(sem(f"moe{l}_add"), n * 2 + 1)
                for g in range(8):
                    if g >= 4:
                        pe.wait_ge(sem("moe_swt"), 8 * l + g - 3)
                    for t in range(TT):
                        x = tp(bank[4 + g % 4][:, P * t:P * t + P], SELW[:, t, P * g:P * g + P], ident)
                    x.then_inc(sem("moe_swtp"), 1)
                for g in range(16):
                    st_, half = g // 2, g % 2
                    if g >= 4:
                        pe.wait_ge(sem("moe_ys"), 16 * l + g - 3)
                    for k in range(4):
                        x = tp(bank[g % 4][:, P * k:P * k + P], YST[:, 4 * half + k, P * st_:P * st_ + P], ident)
                    x.then_inc(sem("moe_ystp"), 1)
                pe.wait_ge(sem("moe_swt"), 8 * l + 8)
                pe.wait_ge(sem("moe_ys"), 16 * l + 16)
                for d in range(KT):
                    if d >= 4:
                        pe.wait_ge(sem("h"), 32 + 16 * l + d - 3)
                    for s in range(8):
                        x = mm(bank[d % 4][:], YS[:, s, P * d:P * d + P], SWT[:, s], start=(s == 0), stop=(s == 7))
                    x.then_inc(sem("moe_f"), 1)

            moe(0)
            norm(5, 2)
            pe.wait_ge(sem("bkt"), 32)
            pe.wait_ge(sem("u"), 48)
            mm(bank[6][0:HEADS2, :], RB[0:BUCKETS], BKT[0:BUCKETS, 0:512], start=True, stop=True)
            mm(bank[7][0:HEADS2, 0:P], RB[0:BUCKETS], BKT[0:BUCKETS, 512:640], start=True, stop=True)\
                .then_inc(sem("vb_mm"), 1)
            def qi(b, w, c0):
                for k in range(KT):
                    x = mm(bank[b][:], w[:, k, c0:c0 + P], U[:, k], start=(k == 0), stop=(k == KT - 1))
                return x

            landed(pe, "b", 0)
            w = chunk("b", 0)
            for t in range(TT):
                for k in range(KT):
                    x = mm(bank[4][:, P * t:P * t + P], U[:, k, P * t:P * t + P], w[:, k, 0:P],
                           start=(k == 0), stop=(k == KT - 1))
            x.then_inc(sem("kv_mm"), 1)
            qi(0, w, P).then_inc(sem("qi_mm"), 1)
            landed(pe, "b", 1)
            qi(1, chunk("b", 1), 0).then_inc(sem("qi_mm"), 1)
            qi(2, chunk("b", 1), P).then_inc(sem("qi_mm"), 1)
            landed(pe, "b", 2)
            w = chunk("b", 2)
            qi(3, w, 0).then_inc(sem("qi_mm"), 1)
            for t in range(TT):
                for k in range(KT):
                    x = mm(bank[5][:, 72 * t:72 * t + 72], U[:, k, P * t:P * t + P], w[:, k, P:200],
                           start=(k == 0), stop=(k == KT - 1))
            x.then_inc(sem("ki_mm"), 1)
            pe.wait_ge(sem("ckv"), 4)
            pe.wait_ge(sem("vb"), 2)
            for t in range(TT):
                x = tp(bank[6][:, P * t:P * t + P], CKV[:, t], ident)
            x.then_inc(sem("kv_tp"), 1)
            pe.wait_ge(sem("ki"), 4)
            for t in range(TT):
                x = tp(bank[7][:, P * t:P * t + P], KI[:, t], ident)
            x.then_inc(sem("kv_tp"), 1)
            pe.wait_ge(sem("kvt"), 2)
            pe.wait_ge(sem("qi"), 4)
            m = 0
            for qb in range(1, TT):
                for h in range(IDX_HEADS):
                    if m >= 4:
                        pe.wait_ge(sem("idx_relu"), m - 3)
                    R = slice(64 * (h % 2), 64 * (h % 2) + 64)
                    n = (qb + 1) * P
                    mm(bank[m % 4][:, 0:n], QI[R, h // 2, P * qb:P * qb + P], KIT[R, 0:n], start=True, stop=True)\
                        .then_inc(sem("idx_mm"), 1)
                    m += 1
            for c in range(8):
                landed(pe, "b", 3 + c)
                for j in range(2):
                    h = 2 * c + j
                    if h >= 4:
                        pe.wait_ge(sem("q2"), h - 3)
                    qi(4 + h % 4, chunk("b", 3 + c), P * j).then_inc(sem("dsa_q"), 1)
            units = [(qb, h) for qb in range(TT) for h in range(HEADS2)]

            def logits(u):
                qb, h = units[u]
                n = (qb + 1) * P
                if u >= 2:
                    pe.wait_ge(sem("ds_s"), u - 1)
                mm(bank[u % 2][:, 0:n], Q2[:, h, qb * P:qb * P + P], CKVT[:, 0:n], start=True, stop=True)\
                    .then_inc(sem("ds_mm"), 1)

            pe.wait_ge(sem("q2"), 16)
            pe.wait_ge(sem("idx_relu"), 24)
            for i in range(len(units) + 3):
                if i < len(units):
                    logits(i)
                if 0 <= i - 2 < len(units):
                    u = i - 2
                    pe.wait_ge(sem("ds_p"), u + 1)
                    if u >= 2:
                        pe.wait_ge(sem("ds_pt"), u - 1)
                    for j in range(units[u][0] + 1):
                        x = tp(bank[2 + u % 2][:, P * j:P * j + P], S2[:, u % 3, P * j:P * j + P], ident)
                    x.then_inc(sem("ds_tp"), 1)
                if i >= 3:
                    u = i - 3
                    qb = units[u][0]
                    pe.wait_ge(sem("ds_pt"), u + 1)
                    if u >= 2:
                        pe.wait_ge(sem("ds_o"), u - 1)
                    for j in range(qb + 1):
                        x = mm(bank[4 + u % 2][:, 0:P], CKV[:, j], PT2[:, u % 2, P * j:P * j + P],
                               start=(j == 0), stop=(j == qb))
                    x.then_inc(sem("ds_pv"), 1)
            pe.wait_ge(sem("ds_o"), 64)
            outproj("dsa_out", HEADS2, UP)
            norm(6, 3)
            moe(1)
            norm(7, 4)
            to_tokens(2, 64)


_WEIGHTS = ["x", "positions", "w_ada", "w_ffn1_in", "w_ffn1_out", "w_in", "w_pool", "w_pool_branch",
            "w_attn_branch", "w_out", "w_ffn2_in", "w_ffn2_out"]
_WEIGHTS2 = ["conv_w_in", "conv_w_out", "attn_w_in", "kv_norm_g", "kidx_ln_g", "kidx_ln_b", "attn_w_out",
             "rel_bias", "router_wg", "router_bg", "router_we", "router_be", "exp_w1", "exp_w3", "exp_w2"]
_SQUEEZE = {"w_ada", "w_ffn1_in", "w_ffn1_out", "w_in", "w_pool", "w_pool_branch", "w_attn_branch", "w_out",
            "w_ffn2_in", "w_ffn2_out", "conv_w_in", "conv_w_out", "attn_w_in", "attn_w_out"}


def kernel(**inputs):
    import numpy as _np
    import concourse.bacc as _bacc
    from concourse import mybir as _mybir
    from concourse.bass_utils import run_bass_kernel_spmd as _run

    nc = _bacc.Bacc("TRN2", target_bir_lowering=False, num_devices=1)
    arrays, A = {}, {}

    def give(name, a):
        a = _np.ascontiguousarray(a)
        arrays[f"in_{name}"] = a
        A[name] = nc.dram_tensor(f"in_{name}", a.shape, _mybir.dt.from_np(a.dtype), kind="ExternalInput").ap()

    for name in _WEIGHTS + _WEIGHTS2:
        a = _np.asarray(inputs[name if name in _WEIGHTS else name + "_2"])
        give(name, a[0] if name in _SQUEEZE else a)
    parts = []
    for name in ("b_ada", "g_norm_ffn1", "g_norm_mix", "g_norm_ffn2", "g_final", "c", "pool_scale",
                 "conv_k_2", "ln1_g_2", "ln1_b_2", "ln2_g_2", "ln2_b_2"):
        parts.append(_np.asarray(inputs[name]).reshape(-1, P).T)
    give("params", _np.concatenate(parts, axis=1))
    give("consts", constants())
    out = nc.dram_tensor("out_0_dram", (1, SEQ, D), F32, kind="ExternalOutput").ap()
    build(nc, A, out)
    r = _run(nc, [arrays], core_ids=[0])
    return r.results[0]["out_0_dram"]
```
